# Optimizing a Trainium2 kernel written in Bass

```python
import jax, jax.numpy as jnp
from jax import lax
import numpy as np
import math

D_MODEL = 1024
BATCH = 1
SEQ = 512
DEPTH = 2

N_MIXERS = 2
N_META = 16
EXPAND = 2
E_POOL = EXPAND * D_MODEL
POOL_WINDOWS = (2, 4, 8, 16)
N_POOL_GROUPS = len(POOL_WINDOWS)
POOL_GROUP_DIM = E_POOL // N_POOL_GROUPS
E_HGRN = EXPAND * D_MODEL
HGRN_HEAD_DIM = 128
N_HGRN_HEADS = E_HGRN // HGRN_HEAD_DIM
CHUNK = 64
PAD_FRONT = (-N_META) % CHUNK
N_POOL_LAYERS = (DEPTH + 1) // 2
N_HGRN_LAYERS = DEPTH // 2
EPS = 1e-6


def rmsnorm(x, w):
    x32 = x.astype(jnp.float32)
    y = x32 * lax.rsqrt(jnp.mean(x32 * x32, axis=-1, keepdims=True) + EPS)
    return (y * w.astype(jnp.float32)).astype(x.dtype)

def pool_mixer(h, w_in, w_grp, scale, w_out):
    b_, L, _ = h.shape
    v, gate = jnp.split(h @ w_in, 2, axis=-1)
    v32 = v.astype(jnp.float32)
    cs = jnp.cumsum(v32, axis=1)
    t = jnp.arange(L)
    groups = []
    for g, w in enumerate(POOL_WINDOWS):
        sl = slice(g * POOL_GROUP_DIM, (g + 1) * POOL_GROUP_DIM)
        c = cs[..., sl]
        c_shift = jnp.pad(c, ((0, 0), (w, 0), (0, 0)))[:, :L]
        cnt = jnp.minimum(t + 1, w).astype(jnp.float32)[None, :, None]
        groups.append((c - c_shift) / cnt - v32[..., sl])
    u = jnp.stack(groups, axis=2).astype(h.dtype)
    u = jnp.einsum('blgc,gcd->blgd', u, w_grp).reshape(b_, L, E_POOL) * scale
    return (u * jax.nn.silu(gate)) @ w_out

def _hgrn_chunk_step(S, xs):
    q, k, v, g = xs
    c = q.shape[2]
    causal = jnp.tril(jnp.ones((c, c), dtype=bool))
    bcum = jnp.cumsum(g, axis=2)
    rel = bcum[:, :, :, None, :] - bcum[:, :, None, :, :]
    decay = jnp.exp(jnp.where(causal[:, :, None], rel, -jnp.inf))
    scores = jnp.einsum('bhtk,bhsk,bhtsk->bhts', q, k, decay)
    o = jnp.einsum('bhts,bhsv->bhtv', scores, v) \
        + jnp.einsum('bhtk,bhkv->bhtv', q * jnp.exp(bcum), S)
    b_end = bcum[:, :, -1, :]
    S_new = jnp.exp(b_end)[..., None] * S \
        + jnp.einsum('bhsk,bhsv->bhkv', k * jnp.exp(b_end[:, :, None, :] - bcum), v)
    return S_new, o

def hgrn2_mixer(h, w_in, lb, o_norm, w_out):
    b_, L, _ = h.shape
    q, fp, i_in, gate = jnp.split(h @ w_in, 4, axis=-1)
    q = jax.nn.silu(q)
    fp32 = fp.astype(jnp.float32)
    lb32 = lb.astype(jnp.float32)
    f = lb32 + (1.0 - lb32) * jax.nn.sigmoid(fp32)
    log_f = jnp.log(f)
    k = (1.0 - lb32) * jax.nn.sigmoid(-fp32)

    def to_chunks(a):
        a = jnp.pad(a.astype(jnp.float32), ((0, 0), (PAD_FRONT, 0), (0, 0)))
        n = a.shape[1] // CHUNK
        return a.reshape(b_, n, CHUNK, N_HGRN_HEADS, HGRN_HEAD_DIM).transpose(1, 0, 3, 2, 4)

    xs = (to_chunks(q), to_chunks(k), to_chunks(i_in), to_chunks(log_f))
    S0 = jnp.zeros((b_, N_HGRN_HEADS, HGRN_HEAD_DIM, HGRN_HEAD_DIM), jnp.float32)
    _, o = lax.scan(_hgrn_chunk_step, S0, xs)
    n = o.shape[0]
    o = o.transpose(1, 0, 3, 2, 4).reshape(b_, n * CHUNK, N_HGRN_HEADS, HGRN_HEAD_DIM)[:, PAD_FRONT:]
    o = o * lax.rsqrt(jnp.mean(o * o, axis=-1, keepdims=True) + EPS)
    o = o.reshape(b_, L, E_HGRN) * o_norm.astype(jnp.float32)
    return (o.astype(h.dtype) * jax.nn.silu(gate)) @ w_out

def first_inputs(seed: int = 0) -> dict:
    key = jax.random.key(seed)
    ks = jax.random.split(key, 12)
    nrm = jax.random.normal
    f32 = jnp.float32
    return {
        "x": nrm(ks[0], (BATCH, SEQ, D_MODEL), f32),
        "meta_tokens": nrm(ks[1], (N_META, D_MODEL), f32),
        "norm_w": 1.0 + 0.05 * nrm(ks[2], (DEPTH, D_MODEL), f32),
        "pool_w_in": nrm(ks[3], (N_POOL_LAYERS, D_MODEL, 2 * E_POOL), f32) * D_MODEL ** -0.5,
        "pool_w_grp": nrm(ks[4], (N_POOL_LAYERS, N_POOL_GROUPS, POOL_GROUP_DIM, POOL_GROUP_DIM), f32) * POOL_GROUP_DIM ** -0.5,
        "pool_scale": 1.0 + 0.1 * nrm(ks[5], (N_POOL_LAYERS, E_POOL), f32),
        "pool_w_out": nrm(ks[6], (N_POOL_LAYERS, E_POOL, D_MODEL), f32) * E_POOL ** -0.5,
        "hgrn_w_in": nrm(ks[7], (N_HGRN_LAYERS, D_MODEL, 4 * E_HGRN), f32) * D_MODEL ** -0.5,
        "hgrn_lb_logits": 1.0 + 0.5 * nrm(ks[8], (DEPTH, E_HGRN), f32),
        "hgrn_o_norm": 1.0 + 0.05 * nrm(ks[9], (N_HGRN_LAYERS, E_HGRN), f32),
        "hgrn_w_out": nrm(ks[10], (N_HGRN_LAYERS, E_HGRN, D_MODEL), f32) * E_HGRN ** -0.5,
        "final_norm_w": 1.0 + 0.05 * nrm(ks[11], (D_MODEL,), f32),
    }

def first_block(x, meta_tokens, norm_w, pool_w_in, pool_w_grp, pool_scale, pool_w_out,
              hgrn_w_in, hgrn_lb_logits, hgrn_o_norm, hgrn_w_out, final_norm_w):
    b_ = x.shape[0]
    meta = jnp.broadcast_to(meta_tokens.astype(x.dtype)[None], (b_, N_META, x.shape[-1]))
    h = jnp.concatenate([meta, x], axis=1)
    p = jax.nn.softmax(hgrn_lb_logits.astype(jnp.float32), axis=0)
    lb_all = jnp.cumsum(p, axis=0) - p[0]
    for i in range(DEPTH):
        hn = rmsnorm(h, norm_w[i])
        j = i // N_MIXERS
        if i % N_MIXERS == 0:
            y = pool_mixer(hn, pool_w_in[j], pool_w_grp[j], pool_scale[j], pool_w_out[j])
        else:
            y = hgrn2_mixer(hn, hgrn_w_in[j], lb_all[i], hgrn_o_norm[j], hgrn_w_out[j])
        h = h + y
    return rmsnorm(h[:, N_META:], final_norm_w)


N_Q_HEADS = 8
N_KV_HEADS = 2
HEAD_DIM = 64
ATTN_WIDTH = N_Q_HEADS * HEAD_DIM
KV_WIDTH = N_KV_HEADS * HEAD_DIM
WINDOW = 128
ATTN_BLOCK = 128
GMLP_GROUPS = 4
GMLP_GROUP_DIM = 128
GMLP_WIDTH = GMLP_GROUPS * GMLP_GROUP_DIM
CHUNK_2 = 128
SPLITS = (ATTN_WIDTH, KV_WIDTH, KV_WIDTH, ATTN_WIDTH,
          GMLP_WIDTH, GMLP_WIDTH, GMLP_WIDTH, D_MODEL, D_MODEL)
IN_WIDTH = sum(SPLITS)
ALPHA = (2 * DEPTH) ** 0.25
BETA = (8 * DEPTH) ** -0.25
LN_EPS = 1e-5


def layer_norm(x, g, b):
    xf = x.astype(jnp.float32)
    mu = xf.mean(-1, keepdims=True)
    var = jnp.square(xf - mu).mean(-1, keepdims=True)
    y = (xf - mu) * lax.rsqrt(var + LN_EPS)
    return (y * g.astype(jnp.float32) + b.astype(jnp.float32)).astype(x.dtype)

def alibi_slopes():
    h = jnp.arange(N_Q_HEADS, dtype=jnp.float32)
    return jnp.exp2(-8.0 * (h + 1.0) / N_Q_HEADS)

def split_columns(h):
    offs = [int(o) for o in np.cumsum(SPLITS)[:-1]]
    return jnp.split(h, offs, axis=-1)

def sliding_window_attention(q, k, v, sinks):
    B, S = q.shape[0], q.shape[1]
    nb = S // ATTN_BLOCK
    grp = N_Q_HEADS // N_KV_HEADS
    qb = q.reshape(B, nb, ATTN_BLOCK, N_KV_HEADS, grp, HEAD_DIM)

    def band(t):
        tb = t.reshape(B, nb, ATTN_BLOCK, N_KV_HEADS, HEAD_DIM)
        prev = jnp.pad(tb, ((0, 0), (1, 0), (0, 0), (0, 0), (0, 0)))[:, :-1]
        return jnp.concatenate([prev, tb], axis=2)

    kb, vb = band(k), band(v)
    scores = jnp.einsum('bnqhgd,bnkhd->bnhgqk', qb, kb).astype(jnp.float32) * (HEAD_DIM ** -0.5)
    qi = jnp.arange(ATTN_BLOCK)[:, None]
    kj = jnp.arange(2 * ATTN_BLOCK)[None, :]
    dist = qi + ATTN_BLOCK - kj
    blk = jnp.arange(nb)[:, None, None]
    key_pos = blk * ATTN_BLOCK + qi - dist
    valid = (dist >= 0) & (dist < WINDOW) & (key_pos >= 0)
    slopes = alibi_slopes().reshape(N_KV_HEADS, grp)
    scores = scores - slopes[:, :, None, None] * dist.astype(jnp.float32)
    scores = jnp.where(valid[None, :, None, None], scores, -jnp.inf)
    sink = sinks.astype(jnp.float32).reshape(N_KV_HEADS, grp)[None, None, :, :, None, None]
    m = jnp.maximum(scores.max(-1, keepdims=True), sink)
    p = jnp.exp(scores - m)
    denom = p.sum(-1, keepdims=True) + jnp.exp(sink - m)
    out = jnp.einsum('bnhgqk,bnkhd->bnqhgd', (p / denom).astype(v.dtype), vb)
    return out.reshape(B, S, ATTN_WIDTH)

def chunked_spatial_gating(u, v, ln_g, ln_b, w_s, b_s):
    B, S = v.shape[0], v.shape[1]
    nc = S // CHUNK_2
    vn = layer_norm(v, ln_g, ln_b).reshape(B, nc, CHUNK_2, GMLP_GROUPS, GMLP_GROUP_DIM)
    causal = jnp.tril(jnp.ones((CHUNK_2, CHUNK_2), dtype=bool))
    w = jnp.where(causal[None], w_s, jnp.zeros_like(w_s))
    mixed = jnp.einsum('gts,bcsgd->bctgd', w, vn) + b_s.T[None, None, :, :, None]
    return u * mixed.reshape(B, S, GMLP_WIDTH)

def second_inputs(seed: int = 0) -> dict:
    key = jax.random.key(seed)
    ks = jax.random.split(key, 16)
    f32 = jnp.float32
    x = jax.random.normal(ks[0], (BATCH, SEQ, D_MODEL), f32)
    w_in = jax.random.normal(ks[1], (DEPTH, D_MODEL, IN_WIDTH), f32) * D_MODEL ** -0.5
    b_in = jax.random.normal(ks[2], (DEPTH, IN_WIDTH), f32) * 0.02
    attn_sinks = jax.random.normal(ks[3], (DEPTH, N_Q_HEADS), f32) * 0.5
    gmlp_ln_g = 1.0 + 0.02 * jax.random.normal(ks[4], (DEPTH, GMLP_WIDTH), f32)
    gmlp_ln_b = 0.02 * jax.random.normal(ks[5], (DEPTH, GMLP_WIDTH), f32)
    w_spatial = jax.random.normal(ks[6], (DEPTH, GMLP_GROUPS, CHUNK_2, CHUNK_2), f32) * (0.5 * CHUNK_2 ** -0.5)
    b_spatial = 1.0 + 0.02 * jax.random.normal(ks[7], (DEPTH, GMLP_GROUPS, CHUNK_2), f32)
    w_branch_attn = jax.random.normal(ks[8], (DEPTH, ATTN_WIDTH, D_MODEL), f32) * (ATTN_WIDTH ** -0.5 * BETA)
    w_branch_gmlp = jax.random.normal(ks[9], (DEPTH, GMLP_WIDTH, D_MODEL), f32) * (GMLP_WIDTH ** -0.5 * BETA)
    w_out = jax.random.normal(ks[10], (DEPTH, D_MODEL, D_MODEL), f32) * (D_MODEL ** -0.5 * BETA)
    b_out = 0.02 * jax.random.normal(ks[11], (DEPTH, D_MODEL), f32)
    ln_g = 1.0 + 0.02 * jax.random.normal(ks[12], (DEPTH, D_MODEL), f32)
    ln_b = 0.02 * jax.random.normal(ks[13], (DEPTH, D_MODEL), f32)
    return {"x": x, "w_in": w_in, "b_in": b_in, "attn_sinks": attn_sinks,
            "gmlp_ln_g": gmlp_ln_g, "gmlp_ln_b": gmlp_ln_b,
            "w_spatial": w_spatial, "b_spatial": b_spatial,
            "w_branch_attn": w_branch_attn, "w_branch_gmlp": w_branch_gmlp,
            "w_out": w_out, "b_out": b_out, "ln_g": ln_g, "ln_b": ln_b}

def second_block(x, w_in, b_in, attn_sinks, gmlp_ln_g, gmlp_ln_b, w_spatial, b_spatial,
              w_branch_attn, w_branch_gmlp, w_out, b_out, ln_g, ln_b):
    B, S = x.shape[0], x.shape[1]
    for l in range(DEPTH):
        h = jnp.einsum('bsd,de->bse', x, w_in[l]) + b_in[l]
        q, k, v, z_a, u_g, v_g, z_g, g_a, g_g = split_columns(h)
        y_a = sliding_window_attention(q.reshape(B, S, N_Q_HEADS, HEAD_DIM),
                                       k.reshape(B, S, N_KV_HEADS, HEAD_DIM),
                                       v.reshape(B, S, N_KV_HEADS, HEAD_DIM),
                                       attn_sinks[l]) * jax.nn.silu(z_a)
        y_g = chunked_spatial_gating(jax.nn.gelu(u_g, approximate=False),
                                     jax.nn.gelu(v_g, approximate=False),
                                     gmlp_ln_g[l], gmlp_ln_b[l],
                                     w_spatial[l], b_spatial[l]) * jax.nn.silu(z_g)
        br_a = jnp.einsum('bse,ed->bsd', y_a, w_branch_attn[l])
        br_g = jnp.einsum('bse,ed->bsd', y_g, w_branch_gmlp[l])
        merged = jax.nn.sigmoid(g_a) * br_a + jax.nn.sigmoid(g_g) * br_g
        out = jnp.einsum('bsd,de->bse', merged, w_out[l]) + b_out[l]
        x = layer_norm(ALPHA * x + out, ln_g[l], ln_b[l])
    return x


def setup_inputs(seed=0):
    out = dict(first_inputs(seed))
    for name, value in second_inputs(seed + 1).items():
        if name != "x":
            out[name + "_2"] = value
    return out


def reference(
    x, meta_tokens, norm_w, pool_w_in, pool_w_grp, pool_scale, pool_w_out, hgrn_w_in,
    hgrn_lb_logits, hgrn_o_norm, hgrn_w_out, final_norm_w, w_in_2, b_in_2, attn_sinks_2,
    gmlp_ln_g_2, gmlp_ln_b_2, w_spatial_2, b_spatial_2, w_branch_attn_2, w_branch_gmlp_2,
    w_out_2, b_out_2, ln_g_2, ln_b_2,
):
    x = first_block(
        x, meta_tokens, norm_w, pool_w_in, pool_w_grp, pool_scale, pool_w_out, hgrn_w_in,
        hgrn_lb_logits, hgrn_o_norm, hgrn_w_out, final_norm_w,
    )
    return second_block(
        x, w_in_2, b_in_2, attn_sinks_2, gmlp_ln_g_2, gmlp_ln_b_2, w_spatial_2, b_spatial_2,
        w_branch_attn_2, w_branch_gmlp_2, w_out_2, b_out_2, ln_g_2, ln_b_2,
    )


_drawn_inputs = setup_inputs


def setup_inputs(seed=0):
    import zlib

    import numpy as np

    out = dict(_drawn_inputs(seed))
    spreads = {}
    factors = {'b_in_2': 8.0,
     'attn_sinks_2': 200.0,
     'gmlp_ln_g_2': 53.878,
     'gmlp_ln_b_2': 50.789,
     'w_spatial_2': 3.029,
     'b_spatial_2': 53.983,
     'b_out_2': 2.807,
     'w_branch_attn_2': 4.01}
    for name, (base, spread) in spreads.items():
        noise = np.random.default_rng([zlib.crc32(name.encode()), seed]).standard_normal(out[name].shape)
        drawn = base * np.exp(spread * noise) if base else spread * noise
        out[name] = __import__('jax').numpy.asarray(drawn.astype(out[name].dtype))
    for name, factor in factors.items():
        out[name] = (out[name] * factor).astype(out[name].dtype)
    return out
```

```python
from contextlib import ExitStack

import concourse.bass as bass
from concourse import mybir

F32 = mybir.dt.float32
F32R = mybir.dt.float32r
I32 = mybir.dt.int32
ALU = mybir.AluOpType
ACT = mybir.ActivationFunctionType
AX_X = mybir.AxisListType.X

P = 128
D = 1024
KT = D // P
META = 16
SEQ = 512
T = META + SEQ
TH = T // 2
NG = 4
GT = 4
E = 2048
NH = E // P
CH = SEQ // P
LEVELS = 7
EPS = 1e-6
LN_EPS = 1e-5
DEPTH = 2
IN2 = 4864
HD = 64
ATT_SCALE = HD ** -0.5
SLOPES = [2.0 ** -(n + 1) for n in range(8)]
ALPHA = (2 * DEPTH) ** 0.25
RAW = 2
PIECES = 4
AHEAD = 3
CREDIT = 2

COL2 = {"q": 0, "k": 4, "v": 5, "za": 6, "u": 10, "vg": 14, "zg": 18, "ga": 22, "gg": 30}
NIN2 = IN2 // P

NW0, NW1, FNW, PSC, ONW, LBA, LBB, N_V1 = 0, 8, 16, 24, 40, 56, 72, 88
BIN, BOUT, LNG, LNB, N_V2 = 0, 76, 92, 108, 124


def plan_a():
    units = []
    for gg in range(2):
        m = 14 * gg
        units += [(gg, "v", n, "k8", m + n, 0) for n in range(4)]
        units += [(gg, "gate", n, "k8", m + 4 + n, 0) for n in range(4)]
        units += [(gg, "grp", n, "k4", m + 8 + n // 2, n % 2) for n in range(4)]
        units += [(gg, "out", n, "k4", m + 10 + n // 2, n % 2) for n in range(8)]
    return units


def plan_c():
    units, m, u = [], 0, 0

    def add(stage, first, count, kind):
        nonlocal m, u
        for n in range(count):
            half = n % 2 if kind == "k4" else 0
            units.append((stage, first + n, kind, m, half, u))
            m += {"k8": 1, "k4": n % 2, "vg": 4}[kind]
            u += 2 if kind == "vg" else 1

    for stage, count in (("q", 4), ("k", 1), ("v", 1), ("za", 4), ("u", 4)):
        add(stage, 0, count, "k8")
    add("vg", 0, 1, "vg")
    add("zg", 0, 4, "k8")
    for half in range(2):
        add("ga", 4 * half, 4, "k8")
        add("gg", 4 * half, 4, "k8")
        add("bra", 4 * half, 4, "k4")
        add("brg", 4 * half, 4, "k4")
    add("wo", 0, 8, "k8")
    return units, m, u


A_PLAN = plan_a()
C_PLAN, C_PIECES, C_UNITS = plan_c()
A_ITERS, A_PIECES, A_UNITS = 2, 28, len(A_PLAN)
PAIR_UNITS = [("f", 0), ("f", 1), ("q", 0), ("q", 1), ("i", 0), ("i", 1), ("g", 0), ("g", 1)]
OUT_UNITS = 8
C_STEPS = C_UNITS + 2

PA, UA = 0, KT
PB, UB = PA + A_ITERS * A_PIECES, UA + A_ITERS * A_UNITS
B_PIECES, B_STEPS = 20, 24
PC, UC = PB + NG * B_PIECES, UB + NG * B_STEPS


def program(nc, a, out):
    with ExitStack() as ctx:
        def sb(name, shape, dt=F32, where=ctx):
            return where.enter_context(nc.sbuf_tensor(name, shape, dt))

        def sem(name):
            return ctx.enter_context(nc.semaphore(name))

        acc = [ctx.enter_context(nc.psum_tensor(f"acc{s}", [P, 2, 512], F32)) for s in range(2)]
        aux = ctx.enter_context(nc.psum_tensor("aux", [P, 2, 512], F32))
        aux2 = ctx.enter_context(nc.psum_tensor("aux2", [P, 2, 512], F32))

        h = sb("h", [P, KT, T])
        xhi = sb("xhi", [P, KT, T], F32R)
        xlo = sb("xlo", [P, KT, T], F32R)
        raw = [sb(f"raw{s}", [P, 2048]) for s in range(RAW)]
        whi = [sb(f"whi{s}", [P, 1024], F32R) for s in range(PIECES)]
        wlo = [sb(f"wlo{s}", [P, 1024], F32R) for s in range(PIECES)]
        ident = sb("ident", [P, P])
        vec1 = sb("vec1", [P, N_V1])
        vec2 = sb("vec2", [P, N_V2])
        ones_d = sb("ones_d", [P, P])
        ones_h = sb("ones_h", [P, P])
        sq = [sb(f"sq{s}", [P, T]) for s in range(2)]
        rstd = sb("rstd", [P, T])
        xn = [sb(f"xn{s}", [P, T]) for s in range(2)]
        lb = sb("lb", [P, NH])
        oml = sb("oml", [P, NH])
        qbias = sb("qbias", [P, DEPTH * 4])

        with ExitStack() as in_a:
            xt = sb("xt", [P, CH, D], where=in_a)
            mt = sb("mt", [META, D], where=in_a)
            rows1 = sb("rows1", [N_V1, P], where=in_a)
            rows2 = sb("rows2", [N_V2, P], where=in_a)
            lbt = sb("lbt", [P, 8, NH], where=in_a)
            vpad = [sb(f"vpad{s}", [P, META + T], where=in_a) for s in range(2)]
            spad = [sb(f"spad{s}", [P, META + T], where=in_a) for s in range(2)]
            pu = [sb(f"pu{s}", [P, T], where=in_a) for s in range(2)]
            uhi = sb("uhi", [P, GT, T], F32R, where=in_a)
            ulo = sb("ulo", [P, GT, T], F32R, where=in_a)
            sga = [sb(f"sga{s}", [P, T], where=in_a) for s in range(2)]
            ga = sb("ga", [P, GT, T], where=in_a)
            pz = [sb(f"pz{s}", [P, T], where=in_a) for s in range(2)]
            zhia = sb("zhia", [P, GT, T], F32R, where=in_a)
            zloa = sb("zloa", [P, GT, T], F32R, where=in_a)
            pool_c = sb("pool_c", [P, NG, 20], where=in_a)

        with ExitStack() as in_b:
            def heads(name, shape):
                return [[sb(f"{name}{p}{x}", shape, where=in_b) for x in range(2)] for p in range(2)]

            fb = heads("fb", [P, T])
            kb = heads("kb", [P, T])
            qb = heads("qb", [P, SEQ])
            ib = heads("ib", [P, T])
            gb = heads("gb", [P, SEQ])
            tb = [{m: sb(f"tb{m}_{x}", [P, T // m if m <= META else SEQ // m], where=in_b)
                   for m in (2, 4, 8, 16, 32, 64, 128)} for x in range(2)]
            sgb = [sb(f"sgb{x}", [P, T], where=in_b) for x in range(2)]
            snb = [sb(f"snb{x}", [P, T], where=in_b) for x in range(2)]
            ab = [sb(f"ab{x}", [P, CH, P], where=in_b) for x in range(2)]
            vt = [sb(f"vt{x}", [P, CH, P], where=in_b) for x in range(2)]
            vtm = [sb(f"vtm{x}", [META, P], where=in_b) for x in range(2)]
            kt = [sb(f"kt{x}", [P, CH - 1, P], where=in_b) for x in range(2)]
            ktm = [sb(f"ktm{x}", [META, P], where=in_b) for x in range(2)]
            st = [sb(f"st{x}", [P, CH, P], where=in_b) for x in range(2)]
            og = [sb(f"og{x}", [P, SEQ], where=in_b) for x in range(2)]
            zhib = sb("zhib", [P, GT, SEQ], F32R, where=in_b)
            zlob = sb("zlob", [P, GT, SEQ], F32R, where=in_b)
            masks = sb("masks", [P, P + 64 * LEVELS], I32, where=in_b)

        in_c = ExitStack()
        nd = sb("nd", [P, 2 * P], where=in_c)
        bvg = sb("bvg", [P, 512], where=in_c)
        gvg = sb("gvg", [P, 512], where=in_c)
        bevg = sb("bevg", [P, 512], where=in_c)
        bsp = sb("bsp", [P, 4, P], where=in_c)
        sinks = sb("sinks", [P, 8], where=in_c)
        wst = sb("wst", [P, 4, P], where=in_c)
        causal = sb("causal", [P, P], where=in_c)
        sm = [sb(f"sm{s}", [P, 8, 2], where=in_c) for s in range(2)]
        vgst = sb("vgst", [P, CH, 8], where=in_c)
        vgr = sb("vgr", [P, CH], where=in_c)
        gac = sb("gac", [P, 4, SEQ], where=in_c)
        ggc = sb("ggc", [P, 4, SEQ], where=in_c)
        with ExitStack() as made_from:
            qc = sb("qc", [P, 4, SEQ], where=made_from)
            za = sb("za", [P, 4, SEQ], where=made_from)
            ug = sb("ug", [P, 4, SEQ], where=made_from)
            zg = sb("zg", [P, 4, SEQ], where=made_from)
        yah = sb("yah", [P, 4, SEQ], F32R, where=in_c)
        yal = sb("yal", [P, 4, SEQ], F32R, where=in_c)
        ygh = sb("ygh", [P, 4, SEQ], F32R, where=in_c)
        ygl = sb("ygl", [P, 4, SEQ], F32R, where=in_c)
        with ExitStack() as before_m:
            kf = sb("kf", [P, SEQ], where=before_m)
            kc = [sb(f"kc{n}", [P, 2, SEQ], where=before_m) for n in range(2)]
            vf = sb("vf", [P, SEQ], where=before_m)
            vtc = sb("vtc", [P, CH, P], where=before_m)
            vn = sb("vn", [P, CH, 512], where=before_m)
            sc = [sb(f"sc{s}", [P, 2, 2 * P], where=before_m) for s in range(2)]
            pr = [sb(f"pr{s}", [P, 2, 2 * P], where=before_m) for s in range(2)]
            pt = [sb(f"pt{s}", [P, 4, P], where=before_m) for s in range(2)]
            sgc = [sb("sgc0", [P, SEQ], where=before_m), rstd[:, 0:SEQ]]
        with ExitStack() as after_m:
            mhi = sb("mhi", [P, KT, SEQ], F32R, where=after_m)
            mlo = sb("mlo", [P, KT, SEQ], F32R, where=after_m)
        in_c.close()
        outt = gac[:, :, :].rearrange("p (s n) t -> p s (n t)", s=2)
        ws = gac[:, 0, :].rearrange("p (g s) -> p g s", g=4)

        raw_landed = [sem(f"raw_landed{s}") for s in range(RAW)]
        hi_ready, lo_ready, lin_done = sem("hi_ready"), sem("lo_ready"), sem("lin_done")
        acc_done = [sem(f"acc_done{s}") for s in range(2)]
        const_landed, x_landed = sem("const_landed"), sem("x_landed")
        c_landed, mask_landed = sem("c_landed"), sem("mask_landed")
        ones_ready, pads_ready = sem("ones_ready"), sem("pads_ready")
        vec_full, vec_ready = sem("vec_full"), sem("vec_ready")
        lb_step, lb_exp = sem("lb_step"), sem("lb_exp")
        sq_ready, sq_used, ms_ready = sem("sq_ready"), sem("sq_used"), sem("ms_ready")
        rstd_ready, xn_ready = sem("rstd_ready"), sem("xn_ready")
        xhi_ready, xlo_ready = sem("xhi_ready"), sem("xlo_ready")
        win_step = sem("win_step")
        uhi_ready, ulo_ready = sem("uhi_ready"), sem("ulo_ready")
        siga_ready = sem("siga_ready")
        zahi_ready, zalo_ready = sem("zahi_ready"), sem("zalo_ready")
        a_zero = sem("a_zero")
        sgb_ready, f_ready, k_ready = sem("sgb_ready"), sem("f_ready"), sem("k_ready")
        vt_full, vt_ready = sem("vt_full"), sem("vt_ready")
        sc_full, sc_done, qk_ready = sem("sc_full"), sem("sc_done"), sem("qk_ready")
        kt_full, kt_ready = sem("kt_full"), sem("kt_ready")
        kv_full, st_ready = sem("kv_full"), sem("st_ready")
        o_full, o2_ready, og_ready = sem("o_full"), sem("o2_ready"), sem("og_ready")
        hm_full, hm_ready, hr_ready = sem("hm_full"), sem("hm_ready"), sem("hr_ready")
        zb_ready, zbhi_ready, zblo_ready = sem("zb_ready"), sem("zbhi_ready"), sem("zblo_ready")
        lc_landed, ws_full, ws_ready = sem("lc_landed"), sem("ws_full"), sem("ws_ready")
        sigc_ready, kd_landed = sem("sigc_ready"), sem("kd_landed")
        kz_ready = sem("kz_ready")
        vtc_full, vtc_ready = sem("vtc_full"), sem("vtc_ready")
        asc_full, asc_ready, arow = sem("asc_full"), sem("asc_ready"), sem("arow")
        aexp, aprob = sem("aexp"), sem("aprob")
        apt_full, apt_ready, ao_full = sem("apt_full"), sem("apt_ready"), sem("ao_full")
        ya_ready, yahi_ready, yalo_ready = sem("ya_ready"), sem("yahi_ready"), sem("yalo_ready")
        vgb_ready, vgg_ready, vgn, vgr_ready = (sem("vgb_ready"), sem("vgg_ready"), sem("vgn"),
                                                sem("vgr_ready"))
        mix_full, yg_step = sem("mix_full"), sem("yg_step")
        yghi_ready, yglo_ready = sem("yghi_ready"), sem("yglo_ready")
        m_ready, mhi_ready, mlo_ready = sem("m_ready"), sem("mhi_ready"), sem("mlo_ready")
        wo_ready, mean_used, xc_ready, ln_t = (sem("wo_ready"), sem("mean_used"), sem("xc_ready"),
                                               sem("ln_t"))
        ot_full, ot_ready, out_sent = sem("ot_full"), sem("ot_ready"), [sem("out_sent0"), sem("out_sent1")]

        passed = {"sp": sem("passed_sp"), "pool": sem("passed_pool"), "dve": sem("passed_dve")}

        def wait_apart(eng, name, *waits):
            for s, v in waits:
                eng.wait_ge(s, v)
            eng.sem_inc(passed[name], 1)

        def raw_view(kind, m):
            slot, q = raw[(m // 2) % RAW], m % 2
            if kind == "vg":
                return slot[:, 1024 * q:1024 * (q + 1)].rearrange("p (k n) -> p k n", k=2)
            w = 128 if kind == "k8" else 256
            return slot[:, :].rearrange("p (k n) -> p k n", n=2 * w)[:, :, q * w:(q + 1) * w]

        def piece(bufs, kind, m):
            return bufs[m % PIECES][:, :].rearrange("p (k n) -> p k n", k={"k8": 8, "k4": 4, "vg": 2}[kind])

        def split_hi(act, kind, m, before, landed, freed):
            act.wait_ge(raw_landed[(m // 2) % RAW], landed)
            if freed is not None:
                act.wait_ge(lin_done, freed)
            act.activation(piece(whi, kind, m), raw_view(kind, m), ACT.Copy).then_inc(hi_ready, 1)

        def split_lo(dve, kind, m, before):
            dve.wait_ge(hi_ready, before + m + 1)
            dve.tensor_tensor(piece(wlo, kind, m), raw_view(kind, m), piece(whi, kind, m),
                              ALU.subtract).then_inc(lo_ready, 1)

        def landed_ab(before, m):
            return before * 4 + 16 * (m // 4 + 1)

        def products(pe, dst, stat, mov, first, last):
            pe.matmul(dst, stat[0], mov[0], start=first, stop=False)
            pe.matmul(dst, stat[0], mov[1], start=False, stop=False)
            return pe.matmul(dst, stat[1], mov[0], start=False, stop=last)

        def unit(pe, slot, kind, m, half, K, rhs, tokens, k_wait=None, mid=None):
            hi, lo = piece(whi, kind, m), piece(wlo, kind, m)
            cols = slice(128 * half, 128 * half + 128)
            parts = [(0, META, SEQ)] if tokens == SEQ else [(0, 0, TH), (1, TH, TH)]
            for n, (bank, t0, w) in enumerate(parts):
                for k in range(K):
                    if n == 0 and k_wait is not None:
                        k_wait(k)
                    mm = products(pe, acc[slot][:, bank, 0:w], (hi[:, k, cols], lo[:, k, cols]),
                                  rhs(k, t0, w), k == 0, k == K - 1)
                    if mid is not None and k == K // 2 - 1 and tokens == SEQ:
                        mid()
                if mid is not None and n == 0 and tokens == T:
                    mid()
            mm.then_inc(lin_done, 1)

        def of_x(k, t0, w):
            return xhi[:, k, t0:t0 + w], xlo[:, k, t0:t0 + w]

        def acc_all(slot):
            return acc[slot][:, :, 0:TH]

        def halves(ap):
            return ap.rearrange("p (b t) -> p b t", b=2)

        def norm_scalar(act, v, tokens, h_ready, final=False):
            t0 = T - tokens
            for k in range(KT):
                h_ready(act, k)
                if k >= 2:
                    act.wait_ge(sq_used, 8 * v + k - 1)
                act.activation(sq[k % 2][:, 0:tokens], h[:, k, t0:T], ACT.Square).then_inc(sq_ready, 1)
            act.wait_ge(ms_ready, 2 * v + 2)
            act.activation(rstd[:, 0:tokens], rstd[:, 0:tokens], ACT.Sqrt).then_inc(rstd_ready, 1)
            for k in range(KT):
                src = h[:, k, t0:T] if final else xn[k % 2][:, 0:tokens]
                act.wait_ge(xn_ready, 8 * v + k + 1)
                act.activation(xhi[:, k, t0:T], src, ACT.Copy).then_inc(xhi_ready, 1)

        def norm_tensor(pe, v, tokens):
            parts = [(1, 0, SEQ)] if tokens == SEQ else [(0, 0, TH), (1, TH, TH)]
            for k in range(KT):
                pe.wait_ge(sq_ready, 8 * v + k + 1)
                for bank, t0, w in parts:
                    mm = pe.matmul(aux[:, bank, 0:w], ones_d[:, :], sq[k % 2][:, t0:t0 + w],
                                   start=(k == 0), stop=(k == KT - 1))
                mm.then_inc(sq_used, 1)

        def inverse_vector(dve, v, src, dst, eps, tokens):
            dve.tensor_scalar(dst, src, eps, None, ALU.add).then_inc(ms_ready, 1)
            dve.wait_ge(ms_ready, 2 * v + 1)
            dve.reciprocal(rstd[:, 0:tokens], rstd[:, 0:tokens]).then_inc(ms_ready, 1)
            dve.wait_ge(rstd_ready, v + 1)

        def norm_vector(dve, v, tokens, wcol, final=False):
            t0 = T - tokens
            dve.wait_ge(sq_used, 8 * v + 8)
            if tokens == SEQ:
                inverse_vector(dve, v, aux[:, 1, :], rstd[:, 0:SEQ], EPS, tokens)
            else:
                inverse_vector(dve, v, aux[:, :, 0:TH], halves(rstd[:, :]), EPS, tokens)

            def scale(k):
                if k >= 2 and not final:
                    dve.wait_ge(xlo_ready, 8 * v + k - 1)
                dst = h[:, k, t0:T] if final else xn[k % 2][:, 0:tokens]
                dve.scalar_tensor_tensor(out=dst, in0=h[:, k, t0:T], scalar=vec1[:, wcol + k:wcol + k + 1],
                                         in1=rstd[:, 0:tokens], op0=ALU.mult, op1=ALU.mult)\
                   .then_inc(xn_ready, 1)

            scale(0)
            for k in range(KT):
                if k + 1 < KT:
                    scale(k + 1)
                src = h[:, k, t0:T] if final else xn[k % 2][:, 0:tokens]
                dve.wait_ge(xhi_ready, 8 * v + k + 1)
                dve.tensor_tensor(xlo[:, k, t0:T], src, xhi[:, k, t0:T], ALU.subtract)\
                   .then_inc(xlo_ready, 1)

        def x_wait(pe, v):
            return lambda k: pe.wait_ge(xlo_ready, 8 * v + k + 1)

        def h_after_out(step0, unit0):
            return lambda eng, k: eng.wait_ge(acc_done[k % 2], unit0 // 2 + k // 2 + 1)

        def qk_after(pair, level, x):
            n = x + 1 if level == 0 else 2 + 6 * (level - 1) + 3 * (x + 1)
            return pair * (2 + 6 * LEVELS) + n

        def second_halves(ap, m):
            return ap.rearrange("p (b two m) -> p b two m", two=2, m=m)[:, :, 1, :]

        def first_halves(ap, m):
            return ap.rearrange("p (b two m) -> p b two m", two=2, m=m)[:, :, 0, :]

        def mask_of(level):
            if level == 0:
                return masks[:, None, 0:P].to_broadcast([P, CH, P])
            m = 2 ** (level - 1)
            cols = masks[:, P + 64 * (level - 1):P + 64 * level].rearrange("p (b m) -> p b m", m=m)
            return cols[:, None, :, :].to_broadcast([P, CH, 64 // m, m])

        STEPS = 6 + LEVELS

        def b_tensor_step(pe, s, pair, par):
            for x in range(2):
                big, small = aux2[:, x, :], aux[:, x, :]
                if s == 0:
                    pe.wait_ge(og_ready, 1 + 2 * pair)
                    pe.wait_ge(hm_ready, 1 + 4 * pair)
                    for c in range(CH):
                        pe.transpose(big[:, P * c:P * c + P],
                                     ib[par][x][:, META + P * c:META + P * c + P], ident[:, :])
                    pe.transpose(small[0:META, 0:P], ib[par][x][:, 0:META], ident[:, :]).then_inc(vt_full, 1)
                elif s <= LEVELS + 1:
                    level = s - 1
                    if level == 0:
                        pe.wait_ge(k_ready, 1 + 2 * pair + x + 1)
                        pe.wait_ge(vt_ready, 4 * pair + 2 * x + 2)
                    else:
                        pe.wait_ge(qk_ready, qk_after(pair, level - 1, x))
                        pe.wait_ge(sc_done, 16 * pair + 2 * (level - 1) + x + 1)
                    m = 2 ** (level - 1) if level else None
                    for c in range(CH):
                        keys = kb[par][x][:, META + P * c:META + P * c + P]
                        q = qb[par][x][:, P * c:P * c + P]
                        if level == 0:
                            dst = small[:, P * c:P * c + P]
                        else:
                            q = second_halves(q, m)
                            dst = small[:, 64 * c:64 * c + 64].rearrange("p (b m) -> p b m", m=m)
                        mm = pe.matmul(dst, keys, q, start=True, stop=True)
                    mm.then_inc(sc_full, 1)
                elif s == LEVELS + 2:
                    pe.wait_ge(qk_ready, qk_after(pair, LEVELS, x))
                    for c in range(CH - 1):
                        pe.transpose(big[:, P * c:P * c + P],
                                     kb[par][x][:, META + P * c:META + P * c + P], ident[:, :])
                    pe.transpose(big[0:META, 3 * P:4 * P], kb[par][x][:, 0:META], ident[:, :])\
                      .then_inc(kt_full, 1)
                elif s == LEVELS + 3:
                    pe.wait_ge(kt_ready, 4 * pair + 2 * x + 2)
                    pe.wait_ge(sc_done, 16 * pair + 14 + x + 1)
                    pe.matmul(small[:, 0:P], ktm[x][:, :], vtm[x][:, :], start=True, stop=True)
                    for c in range(CH - 1):
                        mm = pe.matmul(small[:, P * (c + 1):P * (c + 2)], kt[x][:, c, :], vt[x][:, c, :],
                                       start=True, stop=True)
                    mm.then_inc(kv_full, 1)
                elif s == LEVELS + 4:
                    pe.wait_ge(st_ready, 8 * pair + 4 * x + 4)
                    for c in range(CH):
                        pe.matmul(big[:, P * c:P * c + P], vt[x][:, c, :], ab[x][:, c, :], start=True,
                                  stop=False)
                        mm = pe.matmul(big[:, P * c:P * c + P], st[x][:, c, :],
                                       qb[par][x][:, P * c:P * c + P], start=False, stop=True)
                    mm.then_inc(o_full, 1)
                else:
                    pe.wait_ge(o2_ready, 2 * pair + x + 1)
                    pe.matmul(small, ones_h[:, :], sq[x][:, 0:SEQ], start=True, stop=True)\
                      .then_inc(hm_full, 1)

        def b_vector_step(dve, s, pair, par, group):
            def product(x, out_ap, in_ap, blocks, shape):
                dve.tensor_tensor(out_ap, in_ap, blocks.unsqueeze(2).to_broadcast(shape), ALU.mult)\
                   .then_inc(qk_ready, 1)

            if 1 <= s <= LEVELS + 1:
                level = s - 1
                for x in range(2):
                    waits = [(sc_full, 16 * pair + 2 * level + x + 1)]
                    if level:
                        waits += [(sc_done, 16 * pair + 2 * (level - 1) + x + 1),
                                  (qk_ready, qk_after(pair, level - 1, x))]
                    wait_apart(dve, "dve", *waits)
                    if level == 0:
                        dve.copy_predicated(ab[x][:, :, :], mask_of(0),
                                            aux[:, x, :].rearrange("p (c t) -> p c t", c=CH))\
                           .then_inc(sc_done, 1)
                        dve.tensor_tensor(qb[par][x][:, :], qb[par][x][:, :], fb[par][x][:, META:T],
                                          ALU.mult).then_inc(qk_ready, 1)
                        continue
                    m = 2 ** (level - 1)
                    nb = 64 // m
                    dst = ab[x][:, :, :].rearrange("p c (b two m) -> p c b two m", two=2, m=m)[:, :, :, 1, :]
                    dve.copy_predicated(dst, mask_of(level),
                                        aux[:, x, 0:256].rearrange("p (c b m) -> p c b m", c=CH, m=m))\
                       .then_inc(sc_done, 1)
                    whole = fb[par][x] if m == 1 else tb[x][m]
                    n_meta = META // m if m <= META else 0
                    n_all = n_meta + SEQ // m
                    seq = whole[:, n_meta:n_all].rearrange("p (b two) -> p b two", two=2)
                    q = qb[par][x][:, :]
                    product(x, second_halves(q, m), second_halves(q, m), seq[:, :, 0], [P, CH * nb, m])
                    if m < META:
                        both, k = whole[:, 0:n_all].rearrange("p (b two) -> p b two", two=2), kb[par][x][:, :]
                    else:
                        both, k = seq, kb[par][x][:, META:T]
                    n = n_all // 2 if m < META else SEQ // (2 * m)
                    product(x, first_halves(k, m), first_halves(k, m), both[:, :, 1], [P, n, m])
                    dve.tensor_tensor(tb[x][2 * m][:, 0:n], both[:, :, 0], both[:, :, 1], ALU.mult)\
                       .then_inc(qk_ready, 1)
            elif s == LEVELS + 3:
                for x in range(2):
                    dve.wait_ge(kv_full, 2 * pair + x + 1)
                    dve.tensor_copy(st[x][:, 0, :], aux[:, x, 0:P]).then_inc(st_ready, 1)
                    for c in range(CH - 1):
                        dve.wait_ge(st_ready, 8 * pair + 4 * x + c + 1)
                        dve.scalar_tensor_tensor(out=st[x][:, c + 1, :], in0=st[x][:, c, :],
                                                 scalar=tb[x][128][:, c:c + 1],
                                                 in1=aux[:, x, P * (c + 1):P * (c + 2)],
                                                 op0=ALU.mult, op1=ALU.add).then_inc(st_ready, 1)
            elif s == LEVELS + 4:
                for x in range(2):
                    dve.wait_ge(o2_ready, 2 * pair + x + 1)
                    dve.scalar_tensor_tensor(out=og[x][:, :], in0=aux2[:, x, :],
                                             scalar=vec1[:, bass.ds(ONW + 2 * pair + x, 1)],
                                             in1=gb[par][x][:, :], op0=ALU.mult, op1=ALU.mult)\
                       .then_inc(og_ready, 1)
            elif s == LEVELS + 5:
                for x in range(2):
                    dve.wait_ge(hm_full, 2 * pair + x + 1)
                    dve.tensor_scalar(xn[x][:, 0:SEQ], aux[:, x, :], EPS, None, ALU.add)\
                       .then_inc(hm_ready, 1)
                    dve.wait_ge(hm_ready, 1 + 4 * pair + 2 * x + 1)
                    dve.reciprocal(xn[x][:, 0:SEQ], xn[x][:, 0:SEQ]).then_inc(hm_ready, 1)
                for x in range(2):
                    dve.wait_ge(hr_ready, 2 * pair + x + 1)
                    dve.wait_ge(og_ready, 1 + 2 * pair + x + 1)
                    dve.tensor_tensor(og[x][:, :], og[x][:, :], xn[x][:, 0:SEQ], ALU.mult)\
                       .then_inc(zb_ready, 1)
                for x in range(2):
                    dve.wait_ge(zbhi_ready, 2 * pair + x + 1)
                    dve.tensor_tensor(zlob[:, 2 * par + x, :], og[x][:, :], zhib[:, 2 * par + x, :],
                                      ALU.subtract).then_inc(zblo_ready, 1)

        def b_scalar_step(act, s, pair, par):
            if s == 0:
                for x in range(2):
                    act.wait_ge(vt_full, 2 * pair + x + 1)
                    act.activation(vt[x][:, :, :], aux2[:, x, :].rearrange("p (c d) -> p c d", c=CH),
                                   ACT.Copy).then_inc(vt_ready, 1)
                    act.activation(vtm[x][:, :], aux[0:META, x, 0:P], ACT.Copy).then_inc(vt_ready, 1)
            elif s == LEVELS + 2:
                for x in range(2):
                    act.wait_ge(kt_full, 2 * pair + x + 1)
                    act.activation(kt[x][:, :, :], aux2[:, x, 0:3 * P].rearrange("p (c d) -> p c d", c=3),
                                   ACT.Copy).then_inc(kt_ready, 1)
                    act.activation(ktm[x][:, :], aux2[0:META, x, 3 * P:4 * P], ACT.Copy).then_inc(kt_ready, 1)
            elif s == LEVELS + 4:
                for x in range(2):
                    act.wait_ge(o_full, 2 * pair + x + 1)
                    act.activation(sq[x][:, 0:SEQ], aux2[:, x, :], ACT.Square).then_inc(o2_ready, 1)
            elif s == LEVELS + 5:
                for x in range(2):
                    act.wait_ge(hm_ready, 1 + 4 * pair + 2 * x + 2)
                    act.activation(xn[x][:, 0:SEQ], xn[x][:, 0:SEQ], ACT.Sqrt).then_inc(hr_ready, 1)
                for x in range(2):
                    act.wait_ge(zb_ready, 2 * pair + x + 1)
                    act.activation(zhib[:, 2 * par + x, :], og[x][:, :], ACT.Copy).then_inc(zbhi_ready, 1)

        def pair_units(i, part):
            if part == "first":
                return 0, UB, PB
            k = 0 if part == "odd" else 1
            return 2 * i + 1 + k, UB + 8 + 8 * k + B_STEPS * i, PB + 8 + 8 * k + B_PIECES * i

        def c_base(i):
            return UC + C_STEPS * i

        ATT = [(p, b) for p in range(4) for b in range(CH)]
        STEP_OF = {}
        FREED = {}
        n_steps = 0
        for entry in C_PLAN:
            stage, index, kind, m, half, u = entry
            if kind == "vg":
                for q in range(4):
                    FREED[m + q] = n_steps + q + 1
                n_steps += 4
            else:
                n_steps += 1
                FREED[m] = n_steps
            STEP_OF[stage, index] = n_steps
        C_KIND = {}
        for stage, index, kind, m, half, u in C_PLAN:
            for q in range(4 if kind == "vg" else 1):
                C_KIND[m + q] = kind

        def c_done(i, u):
            return UC // 2 + (C_UNITS // 2) * i + u // 2 + 1

        def c_slots():
            att = pv = 0
            order = []
            for entry in C_PLAN:
                stage, index, kind, m, half, u = entry
                for q in range(4 if kind == "vg" else 1):
                    side = []
                    if stage == "za" and index == 0:
                        side.append(("vtc", 0))
                        side.append(("ws", 0))
                    elif att < len(ATT) and stage in ("za", "u", "vg", "zg", "ga", "gg"):
                        side.append(("att", att))
                        att += 1
                    elif att < len(ATT) + 2 and att >= len(ATT):
                        side.append(("att", att))
                        att += 1
                    if stage in ("gg",) and index < 4:
                        side.append(("mix", index))
                    order.append((entry, q, side))
            return order

        C_ORDER = c_slots()

        block = ctx.enter_context(nc.Block())

        def load_chunk(sp, n, slot, src, kind, value):
            wait_apart(sp, "sp", (lo_ready, value))
            w = 256 if kind == "k8" else 512
            sp.dma_start(raw[slot][:, :].rearrange("p (k n) -> p k n", n=w), src)\
              .then_inc(raw_landed[slot], 16)

        w_in_a = a["pool_w_in"][0].rearrange("(k p) n -> p k n", p=P)
        w_grp = a["pool_w_grp"][0].rearrange("g (k p) n -> p (g k) n", p=P)
        w_out_a = a["pool_w_out"][0].rearrange("(k p) n -> p k n", p=P)
        w_in_b = a["hgrn_w_in"][0].rearrange("(k p) n -> p k n", p=P)
        w_out_b = a["hgrn_w_out"][0].rearrange("(k p) n -> p k n", p=P)
        w_in_c = a["w_in_2"].rearrange("l (k p) n -> p (l k) n", p=P)
        w_bra = a["w_branch_attn_2"].rearrange("l (k p) n -> p (l k) n", p=P)
        w_brg = a["w_branch_gmlp_2"].rearrange("l (k p) n -> p (l k) n", p=P)
        w_out_c = a["w_out_2"].rearrange("l (k p) n -> p (l k) n", p=P)

        @block.sync
        def _(sp):
            def const(dst, src):
                sp.dma_start(dst, src).then_inc(const_landed, 16)

            const(ident[:, :], a["c_ident"])
            const(rows1[NW0:FNW, :], a["norm_w"].rearrange("l (k p) -> (l k) p", p=P))
            const(rows1[FNW:PSC, :], a["final_norm_w"].rearrange("(k p) -> k p", p=P))
            const(rows1[PSC:ONW, :], a["pool_scale"].rearrange("l (k p) -> (l k) p", p=P))
            const(rows1[ONW:LBA, :], a["hgrn_o_norm"].rearrange("l (k p) -> (l k) p", p=P))
            const(rows1[LBA:N_V1, :], a["hgrn_lb_logits"].rearrange("l (k p) -> (l k) p", p=P))
            const(rows2[BIN:BOUT, :], a["b_in_2"].rearrange("l (k p) -> (l k) p", p=P))
            const(rows2[BOUT:LNG, :], a["b_out_2"].rearrange("l (k p) -> (l k) p", p=P))
            const(rows2[LNG:LNB, :], a["ln_g_2"].rearrange("l (k p) -> (l k) p", p=P))
            const(rows2[LNB:N_V2, :], a["ln_b_2"].rearrange("l (k p) -> (l k) p", p=P))
            const(pool_c[:, :, :], a["c_pool"])
            for c in range(CH):
                sp.dma_start(xt[:, c, :], a["x"][0][P * c:P * c + P, :]).then_inc(x_landed, 16)
            sp.dma_start(mt[:, :], a["meta_tokens"]).then_inc(x_landed, 16)

            with sp.Fori(0, A_ITERS) as i:
                n = 0
                for gg in range(2):
                    g = 2 * i + gg
                    srcs = [("k8", w_in_a[:, :, bass.ds(512 * g + 256 * c, 256)]) for c in range(2)]
                    srcs += [("k8", w_in_a[:, :, bass.ds(E + 512 * g + 256 * c, 256)]) for c in range(2)]
                    srcs += [("k4", w_grp[:, bass.ds(GT * g, GT), :])]
                    srcs += [("k4", w_out_a[:, bass.ds(GT * g, GT), 512 * c:512 * c + 512]) for c in range(2)]
                    for kind, src in srcs:
                        load_chunk(sp, n, n % 2, src, kind, PA + A_PIECES * i + 2 * n - 2 + CREDIT)
                        n += 1

            def load_pair(i, part):
                pair, _, before = pair_units(i, part)
                for n, col in enumerate((E, 0, 2 * E, 3 * E)):
                    load_chunk(sp, n, n % 2, w_in_b[:, :, bass.ds(col + 256 * pair, 256)], "k8",
                               before + 2 * n - 2 + CREDIT)

            def load_out_b(g, before):
                for n in range(2):
                    load_chunk(sp, n, n % 2, w_out_b[:, bass.ds(GT * g, GT), 512 * n:512 * n + 512], "k4",
                               before + 2 * n - 2 + CREDIT)

            load_pair(None, "first")
            sp.wait_ge(xlo_ready, 16)
            sp.dma_start(masks[:, :], a["c_masks"]).then_inc(mask_landed, 16)
            with sp.Fori(0, NG - 1) as i:
                load_pair(i, "odd")
                load_pair(i, "even")
                load_out_b(i, PB + 24 + B_PIECES * i)
            load_pair(NG - 1, "odd")
            load_out_b(NG - 1, PB + 16 + B_PIECES * (NG - 1))

            with sp.Fori(0, DEPTH) as i:
                before = PC + C_PIECES * i
                chunks = []
                for stage, index, kind, m, half, u in C_PLAN:
                    if half or m % 2:
                        continue
                    if kind == "vg":
                        for c in range(2):
                            chunks.append((kind, w_in_c[:, bass.ds(8 * i + 4 * c, 4),
                                                        P * COL2["vg"]:P * COL2["vg"] + 512]))
                    elif stage == "wo":
                        chunks.append((kind, w_out_c[:, bass.ds(8 * i, 8), P * index:P * index + 256]))
                    elif kind == "k4":
                        src = w_bra if stage == "bra" else w_brg
                        chunks.append((kind, src[:, bass.ds(4 * i, 4), P * index:P * index + 512]))
                    else:
                        col = P * (COL2[stage] + index)
                        chunks.append((kind, w_in_c[:, bass.ds(8 * i, 8), col:col + 256]))
                for n, (kind, src) in enumerate(chunks):
                    value = before + CREDIT if n < 2 else before + 2 * n - 2 + CREDIT
                    load_chunk(sp, n, n % 2, src, kind, value)

            for c in range(CH):
                sp.wait_ge(ot_ready, 2 * c + 2)
                sp.dma_start(out[0][P * c:P * c + P, :], outt[:, c % 2, :]).then_inc(out_sent[c % 2], 16)
            for s in range(2):
                sp.wait_ge(out_sent[s], 16 * (CH // 2))

        @block.gpsimd
        def _(pool):
            pool.memset(ones_d[:, :], 1.0 / D).then_inc(ones_ready, 1)
            pool.memset(ones_h[:, :], 1.0 / P).then_inc(ones_ready, 1)
            for buf in vpad + spad:
                pool.memset(buf[:, 0:META], 0.0).then_inc(pads_ready, 1)
            pool.wait_ge(xlo_ready, 16)
            for x in range(2):
                pool.memset(ab[x][:, :, :], 0.0).then_inc(a_zero, 1)
            pool.wait_ge(xlo_ready, 24)
            pool.dma_start(nd[:, :], a["c_nd"]).then_inc(c_landed, 16)
            pool.dma_start(causal[:, :], a["c_causal"]).then_inc(c_landed, 16)
            with pool.Fori(0, DEPTH) as i:
                wait_apart(pool, "pool", (lin_done, c_base(i)))

                def rows(dst, src):
                    pool.dma_start(dst, src).then_inc(lc_landed, 16)

                def row(name, w):
                    return a[name][bass.ds(i, 1), :].to_broadcast([P, w])

                rows(ws, a["w_spatial_2"].rearrange("l g t s -> t (l g) s")[:, bass.ds(4 * i, 4), :])
                rows(bvg[:, :], a["b_in_2"][bass.ds(i, 1), P * COL2["vg"]:P * COL2["vg"] + 512]
                     .to_broadcast([P, 512]))
                rows(gvg[:, :], row("gmlp_ln_g_2", 512))
                rows(bevg[:, :], row("gmlp_ln_b_2", 512))
                rows(bsp[:, :, :].rearrange("p g t -> p (g t)"),
                     a["b_spatial_2"].rearrange("l g t -> l (g t)")[bass.ds(i, 1), :].to_broadcast([P, 512]))
                rows(sinks[:, :], row("attn_sinks_2", 8))
                for kv in range(2):
                    for x in range(2):
                        pool.memset(kc[kv][HD * x:HD * x + HD, 1 - x, :], 0.0).then_inc(kz_ready, 1)
                wait_apart(pool, "pool", (acc_done[0], c_done(i, 4)))
                for kv in range(2):
                    for x in range(2):
                        pool.dma_start(kc[kv][HD * x:HD * x + HD, x, :], kf[HD * kv:HD * kv + HD, :])\
                            .then_inc(kd_landed, 16)

        @block.tensor
        def _(pe):
            pe.wait_ge(const_landed, 16 * 11)
            pe.transpose(aux2[:, 0, 0:N_V1], rows1[:, :], ident[0:N_V1, 0:N_V1]).then_inc(vec_full, 1)
            pe.transpose(aux2[:, 1, 0:N_V2], rows2[:, :], ident[0:N_V2, 0:N_V2]).then_inc(vec_full, 1)
            pe.wait_ge(x_landed, 16 * (CH + 1))
            for k in range(KT):
                pe.wait_ge(acc_done[k % 2], k // 2)
                for c in range(CH):
                    pe.transpose(acc[k % 2][:, 0, P * c:P * c + P], xt[:, c, P * k:P * k + P], ident[:, :])
                pe.transpose(acc[k % 2][:, 1, 0:META], mt[:, P * k:P * k + P], ident[0:META, 0:META])\
                  .then_inc(lin_done, 1)
            pe.wait_ge(ones_ready, 2)
            norm_tensor(pe, 0, T)

            with pe.Fori(0, A_ITERS) as i:
                for u, (gg, stage, n, kind, m, half) in enumerate(A_PLAN):
                    G = 2 * i + gg
                    pe.wait_ge(acc_done[u % 2], UA // 2 + (A_UNITS // 2) * i + u // 2)
                    pe.wait_ge(lo_ready, PA + A_PIECES * i + m + 1 + CREDIT)
                    if stage == "grp":
                        rhs = lambda k, t0, w: (uhi[:, k, t0:t0 + w], ulo[:, k, t0:t0 + w])
                        k_wait = (lambda k: pe.wait_ge(ulo_ready, 4 * G + k + 1)) if n == 0 else None
                    elif stage == "out":
                        rhs = lambda k, t0, w: (zhia[:, k, t0:t0 + w], zloa[:, k, t0:t0 + w])
                        k_wait = (lambda k: pe.wait_ge(zalo_ready, 4 * G + k + 1)) if n == 0 else None
                    else:
                        rhs, k_wait = of_x, (x_wait(pe, 0) if u == 0 else None)
                    unit(pe, u % 2, kind, m, half, KT if kind == "k8" else GT, rhs, T, k_wait)
            norm_tensor(pe, 1, T)

            def b_pair(i, part, process):
                pair, u0, p0 = pair_units(i, part)
                slot = 0

                def side():
                    nonlocal slot
                    if process is not None and 1 <= slot <= STEPS:
                        b_tensor_step(pe, slot - 1, *process)
                    slot += 1

                for j, (what, x) in enumerate(PAIR_UNITS):
                    pe.wait_ge(acc_done[x], u0_half(part, i) + j // 2)
                    pe.wait_ge(lo_ready, p0 + j + 1 + CREDIT)
                    unit(pe, x, "k8", j, 0, KT, of_x, T if what in "fi" else SEQ,
                         x_wait(pe, 1) if part == "first" and j == 0 else None, side)
                    side()

            def u0_half(part, i):
                if part == "first":
                    return UB // 2
                return UB // 2 + (4 if part == "odd" else 8) + (B_STEPS // 2) * i

            def b_out(g, u0h, p0):
                z = lambda k, t0, w: (zhib[:, k, :], zlob[:, k, :])
                for n in range(OUT_UNITS):
                    pe.wait_ge(acc_done[n % 2], u0h + n // 2)
                    pe.wait_ge(lo_ready, p0 + n // 2 + 1 + CREDIT)
                    unit(pe, n % 2, "k4", n // 2, n % 2, GT, z, SEQ,
                         (lambda k: pe.wait_ge(zblo_ready, 4 * g + k + 1)) if n == 0 else None)

            b_pair(None, "first", None)
            pe.wait_ge(a_zero, 2)
            with pe.Fori(0, NG - 1) as i:
                b_pair(i, "odd", (2 * i, 0))
                b_pair(i, "even", (2 * i + 1, 1))
                b_out(i, UB // 2 + 12 + (B_STEPS // 2) * i, PB + 24 + B_PIECES * i)
            b_pair(NG - 1, "odd", (2 * (NG - 1), 0))
            for s in range(STEPS):
                b_tensor_step(pe, s, 2 * NG - 1, 1)
            b_out(NG - 1, UB // 2 + 8 + (B_STEPS // 2) * (NG - 1), PB + 16 + B_PIECES * (NG - 1))
            norm_tensor(pe, 2, SEQ)

            def att_tensor(i, s):
                base = 16 * i
                if s < len(ATT):
                    p, b = ATT[s]
                    if s == 0:
                        pe.wait_ge(kd_landed, 64 * i + 64)
                        pe.wait_ge(kz_ready, 4 * i + 4)
                        pe.wait_ge(ws_ready, i + 1)
                    pe.wait_ge(asc_ready, 1 + 2 * (base + s))
                    lo = 0 if b else P
                    pe.matmul(aux[:, 0, :].rearrange("p (x k) -> p x k", x=2)[:, :, lo:],
                              qc[:, p, P * b:P * b + P], kc[p // 2][:, :, P * (b - 1) + lo:P * (b + 1)],
                              start=True, stop=True).then_inc(asc_full, 1)
                if 1 <= s <= len(ATT):
                    b = ATT[s - 1][1]
                    pe.wait_ge(aprob, 4 * (base + s - 1) + 4)
                    pe.wait_ge(apt_ready, 1 + base + s - 1)
                    for x in range(2):
                        for kb_ in range(0 if b else 1, 2):
                            mm = pe.transpose(aux2[:, 0, P * (2 * x + kb_):P * (2 * x + kb_ + 1)],
                                              pr[(s - 1) % 2][:, x, P * kb_:P * kb_ + P], ident[:, :])
                    mm.then_inc(apt_full, 1)
                if 2 <= s:
                    p, b = ATT[s - 2]
                    pe.wait_ge(apt_ready, 1 + base + s - 1)
                    if b == 0:
                        pe.wait_ge(ya_ready, 1 + 4 * i + p)
                    for x in range(2):
                        kv = (2 * p + x) // 4
                        for kb_ in range(0 if b else 1, 2):
                            mm = pe.matmul(aux2[HD * x:HD * x + HD, 1, P * b:P * b + P],
                                           vtc[:, b - 1 + kb_, HD * kv:HD * kv + HD],
                                           pt[(s - 2) % 2][:, 2 * x + kb_, :],
                                           start=(kb_ == (0 if b else 1)), stop=(kb_ == 1))
                    mm.then_inc(ao_full, 1)

            def side_tensor(i, what, n):
                if what == "vtc":
                    pe.wait_ge(acc_done[1], c_done(i, 5))
                    for c in range(CH):
                        mm = pe.transpose(aux2[:, 0, P * c:P * c + P], vf[:, P * c:P * c + P], ident[:, :])
                    mm.then_inc(vtc_full, 1)
                elif what == "ws":
                    pe.wait_ge(lc_landed, 96 * i + 96)
                    for g in range(4):
                        mm = pe.transpose(aux2[:, 1, P * g:P * g + P], ws[:, g, :], ident[:, :])
                    mm.then_inc(ws_full, 1)
                elif what == "att":
                    if n == 0:
                        pe.wait_ge(vtc_ready, i + 1)
                    att_tensor(i, n)
                else:
                    pe.wait_ge(vgn, 22 * i + 22)
                    pe.wait_ge(yg_step, 1 + 12 * i + 3 * n)
                    for c in range(CH):
                        mm = pe.matmul(aux[:, 1, P * c:P * c + P], vn[:, c, P * n:P * n + P], wst[:, n, :],
                                       start=True, stop=True)
                    mm.then_inc(mix_full, 1)

            def mean_part(i, k):
                pe.wait_ge(wo_ready, 8 * i + k + 1)
                pe.matmul(aux[:, 1, :], ones_d[:, :], h[:, k, META:T], start=(k == 0),
                          stop=(k == KT - 1)).then_inc(mean_used, 1)

            with pe.Fori(0, DEPTH) as i:
                for (stage, index, kind, m, half, u), q, side in C_ORDER:
                    if q == 0:
                        pe.wait_ge(acc_done[u % 2], c_done(i, u) - 1)
                    pe.wait_ge(lo_ready, PC + C_PIECES * i + m + q + 1 + CREDIT)
                    if stage == "vg":
                        if q == 0:
                            pe.wait_ge(acc_done[1], c_done(i, u + 1) - 1)
                        hi, lo = piece(whi, kind, m + q), piece(wlo, kind, m + q)
                        for c in range(CH):
                            for kk in range(2):
                                k, t0 = 2 * q + kk, META + P * c
                                mm = products(pe, acc[c // 2][:, c % 2, :],
                                              (xhi[:, k, t0:t0 + P], xlo[:, k, t0:t0 + P]),
                                              (hi[:, kk, :], lo[:, kk, :]), k == 0, k == KT - 1)
                        mm.then_inc(lin_done, 1)
                    else:
                        k_wait = None
                        if stage in ("bra", "brg"):
                            y, ready = ((yah, yal), yalo_ready) if stage == "bra" else ((ygh, ygl), yglo_ready)
                            rhs = lambda k, t0, w: (y[0][:, k, :], y[1][:, k, :])
                            if index == 0:
                                k_wait = lambda k: pe.wait_ge(ready, 4 * i + k + 1)
                        elif stage == "wo":
                            rhs = lambda k, t0, w: (mhi[:, k, :], mlo[:, k, :])
                            if index == 0:
                                k_wait = lambda k: pe.wait_ge(mlo_ready, 8 * i + k + 1)
                        else:
                            rhs = of_x
                            if u == 0:
                                k_wait = lambda k: pe.wait_ge(xlo_ready, 16 + 8 * i + k + 1)
                        unit(pe, u % 2, kind, m, half, GT if kind == "k4" else KT, rhs, SEQ, k_wait)
                        if stage == "wo" and index:
                            mean_part(i, index - 1)
                    for what, n in side:
                        side_tensor(i, what, n)
                mean_part(i, KT - 1)
                for k in range(KT):
                    pe.wait_ge(sq_ready, 24 + 8 * i + k + 1)
                    pe.matmul(aux[:, 0, :], ones_d[:, :], sq[k % 2][:, 0:SEQ], start=(k == 0),
                              stop=(k == KT - 1)).then_inc(sq_used, 1)

            pe.wait_ge(xn_ready, 24 + 8 * DEPTH)
            for c in range(CH):
                pe.wait_ge(ot_ready, max(0, 2 * (c - 1)))
                for k in range(KT):
                    mm = pe.transpose(acc[c % 2][:, k // 4, P * (k % 4):P * (k % 4) + P],
                                      h[:, k, META + P * c:META + P * c + P], ident[:, :])
                mm.then_inc(ot_full, 1)

        @block.scalar
        def _(act):
            act.sem_inc(apt_ready, 1)
            act.wait_ge(lb_step, 3)
            act.activation(lbt[:, 3:5, :], lbt[:, 1:3, :], ACT.Exp).then_inc(lb_exp, 1)
            for k in range(KT):
                act.wait_ge(lin_done, k + 1)
                act.activation(h[:, k, META:T], acc[k % 2][:, 0, :], ACT.Copy)
                act.activation(h[:, k, 0:META], acc[k % 2][:, 1, 0:META], ACT.Copy)\
                   .then_inc(acc_done[k % 2], 1)
            norm_scalar(act, 0, T, lambda e, k: e.wait_ge(acc_done[k % 2], k // 2 + 1))
            for m in range(AHEAD):
                split_hi(act, "k8", m, PA, landed_ab(PA, m), None)

            def a_split(i, m):
                m += AHEAD
                kinds = (["k8"] * 8 + ["k4"] * 6) * 2 + ["k8"] * AHEAD
                freed = [max(n + 1 for n, e in enumerate(A_PLAN) if e[4] == f) for f in range(A_PIECES)]
                at = freed[m - PIECES] if m >= PIECES else m - PIECES + 1
                split_hi(act, kinds[m], m, None, 4 * PA + 4 * A_PIECES * i + 16 * (m // 4 + 1),
                         UA + A_UNITS * i + at)

            def u_hi(G, n):
                act.wait_ge(win_step, 1 + 24 * G + 6 * n + 6)
                act.activation(uhi[:, n, :], pu[n % 2][:, :], ACT.Copy).then_inc(uhi_ready, 1)

            with act.Fori(0, A_ITERS) as i:
                for u, (gg, stage, n, kind, m, half) in enumerate(A_PLAN):
                    G, slot = 2 * i + gg, u % 2
                    if stage != "out":
                        act.wait_ge(lin_done, UA + A_UNITS * i + u + 1)
                    if stage == "v":
                        act.wait_ge(win_step, 1 + 24 * G + 6 * max(n - 1, 0))
                        if n == 0:
                            act.wait_ge(pads_ready, 4)
                        act.activation(halves(vpad[slot][:, META:META + T]), acc_all(slot), ACT.Copy)\
                           .then_inc(acc_done[slot], 1)
                    elif stage == "gate":
                        act.activation(halves(sga[slot][:, :]), acc_all(slot), ACT.Sigmoid)\
                           .then_inc(siga_ready, 1)
                    last_of_piece = kind == "k8" or half == 1
                    if last_of_piece:
                        a_split(i, m)
                    if stage == "v" and n or stage == "gate" and n == 0:
                        u_hi(G, (n - 1) % 4)
                    if stage == "grp":
                        act.wait_ge(acc_done[slot], UA // 2 + (A_UNITS // 2) * i + u // 2 + 1)
                        act.activation(zhia[:, n, :], pz[slot][:, :], ACT.Copy).then_inc(zahi_ready, 1)
            norm_scalar(act, 1, T, lambda e, k: e.wait_ge(acc_done[k % 2], UB // 2 - 4 + k // 2 + 1))

            B_KINDS = ["k8"] * 16 + ["k4"] * 4

            def b_split(p0, m, kind, freed):
                split_hi(act, kind, m % 4, None, 4 * p0 + 16 * (m // 4 + 1), freed)

            def b_pair(i, part, process, after):
                pair, u0, p0 = pair_units(i, part)
                slot = 0

                def side():
                    nonlocal slot
                    if process is not None and 1 <= slot <= STEPS:
                        b_scalar_step(act, slot - 1, *process)
                    slot += 1

                for j, (what, x) in enumerate(PAIR_UNITS):
                    side()
                    act.wait_ge(lin_done, u0 + j + 1)
                    if what == "f":
                        act.wait_ge(k_ready, 1 + 2 * pair)
                        act.activation(halves(sgb[x][:, :]), acc_all(x), ACT.Sigmoid).then_inc(sgb_ready, 1)
                        act.activation(halves(snb[x][:, :]), acc_all(x), ACT.Sigmoid, scale=-1.0)\
                           .then_inc(acc_done[x], 1)
                    elif what == "i":
                        act.activation(halves(ib[part == "odd"][x][:, :]), acc_all(x), ACT.Copy)\
                           .then_inc(acc_done[x], 1)
                    else:
                        if what == "q":
                            act.wait_ge(f_ready, 2 * pair + x + 1)
                        act.activation(sgb[x][:, 0:SEQ], acc[x][:, 0, :], ACT.Sigmoid).then_inc(sgb_ready, 1)
                    m = j + AHEAD
                    b_split(p0, m, "k8" if m < 8 else after, u0 + m - 3)
                    side()

            def b_out_splits(u0, p0, ahead):
                for n in range(1, OUT_UNITS, 2):
                    m = n // 2 + AHEAD
                    if m < 4 or ahead:
                        act.wait_ge(lin_done, u0 + n + 1)
                        freed = u0 if m == 3 else u0 + 2 * (m - 3)
                        b_split(p0, m, "k4" if m < 4 else "k8", freed)

            b_pair(None, "first", None, "k8")
            with act.Fori(0, NG - 1) as i:
                b_pair(i, "odd", (2 * i, 0), "k8")
                b_pair(i, "even", (2 * i + 1, 1), "k4")
                b_out_splits(UB + 24 + B_STEPS * i, PB + 24 + B_PIECES * i, True)
            b_pair(NG - 1, "odd", (2 * (NG - 1), 0), "k4")
            for s in range(STEPS):
                b_scalar_step(act, s, 2 * NG - 1, 1)
            b_out_splits(UB + 16 + B_STEPS * (NG - 1), PB + 16 + B_PIECES * (NG - 1), False)
            norm_scalar(act, 2, SEQ, lambda e, k: e.wait_ge(acc_done[k % 2], UC // 2 - 4 + k // 2 + 1),
                        final=True)

            def c_split(i, m):
                landed = 4 * PC + 16 * (m // 4 + 1) + (16 * 14 if (m // 2) % 2 == 0 else 16 * 13) * i
                freed = c_base(i) + (FREED[m - PIECES] if m >= PIECES else 0)
                split_hi(act, C_KIND[m], m, None, landed, freed)

            def att_scalar(i, s):
                base = 16 * i
                if s < len(ATT):
                    p, b = ATT[s]
                    lo, z = (0 if b else P), s % 2
                    act.wait_ge(arow, 4 * (base + s) + 4)
                    for x in range(2):
                        act.activation(pr[z][:, x, lo:], sc[z][:, x, lo:], ACT.Exp,
                                       bias=sm[z][:, 2, x:x + 1], accum_out=sm[z][:, 4, x:x + 1])\
                           .then_inc(aexp, 1)
                    act.activation(sm[z][:, 5, :], sm[z][:, 3, :], ACT.Exp).then_inc(aexp, 1)

            def att_scalar_turned(i, s):
                if 1 <= s <= len(ATT):
                    b = ATT[s - 1][1]
                    act.wait_ge(apt_full, 16 * i + s)
                    z, first = (s - 1) % 2, (0 if b else 1)
                    act.activation(pt[z][:, :, :].rearrange("p (x k) q -> p x k q", x=2)[:, :, first:, :],
                                   aux2[:, 0, :].rearrange("p (x k q) -> p x k q", x=2, k=2)[:, :, first:, :],
                                   ACT.Copy).then_inc(apt_ready, 1)
                if s >= 2 and ATT[s - 2][1] == CH - 1:
                    p = ATT[s - 2][0]
                    act.wait_ge(ya_ready, 1 + 4 * i + p + 1)
                    act.activation(yah[:, p, :], sq[p % 2][:, 0:SEQ], ACT.Copy).then_inc(yahi_ready, 1)

            with act.Fori(0, DEPTH) as i:
                def bias(col):
                    return vec2[:, bass.ds(NIN2 * i + col, 1)]

                for m in range(AHEAD):
                    c_split(i, m)
                for (stage, index, kind, m, half, u), q, side in C_ORDER:
                    slot, n = u % 2, index % 4
                    psum = acc[slot][:, 0, :]
                    b = bias(COL2[stage] + index) if stage in COL2 else None
                    step = STEP_OF[stage, index] - (3 - q if stage == "vg" else 0)
                    if stage not in ("bra", "brg"):
                        act.wait_ge(lin_done, c_base(i) + step)
                    if stage == "q":
                        act.activation(qc[:, n, :], psum, ACT.Identity, scale=ATT_SCALE,
                                       bias=qbias[:, bass.ds(4 * i + n, 1)]).then_inc(acc_done[slot], 1)
                    elif stage in ("k", "v"):
                        act.activation((kf if stage == "k" else vf)[:, :], psum, ACT.Identity, bias=b)\
                           .then_inc(acc_done[slot], 1)
                    elif stage in ("za", "zg"):
                        act.activation(sgc[slot][:, :], psum, ACT.Sigmoid, bias=b).then_inc(sigc_ready, 1)
                    elif stage == "u":
                        act.activation(ug[:, n, :], psum, ACT.Gelu, bias=b).then_inc(acc_done[slot], 1)
                    elif stage == "vg" and q == 3:
                        for c in range(CH):
                            if c % 2 == 0:
                                act.wait_ge(vgb_ready, 2 * i + c // 2 + 1)
                            else:
                                act.wait_ge(acc_done[c // 2], c_done(i, u + c // 2))
                            act.activation(vn[:, c, :], vn[:, c, :], ACT.Gelu).then_inc(vgg_ready, 1)
                    elif stage in ("ga", "gg"):
                        if index == 4:
                            act.wait_ge(mlo_ready, 8 * i + 4)
                        act.activation((gac if stage == "ga" else ggc)[:, n, :], psum, ACT.Sigmoid, bias=b)\
                           .then_inc(acc_done[slot], 1)
                    elif stage == "wo":
                        if index >= 2:
                            act.wait_ge(wo_ready, 8 * i + index - 1)
                        act.activation(xn[slot][:, 0:SEQ], psum, ACT.Identity,
                                       bias=vec2[:, bass.ds(BOUT + 8 * i + index, 1)])\
                           .then_inc(acc_done[slot], 1)
                    for what, s in side:
                        if what == "att":
                            att_scalar(i, s)
                    if kind != "k4" or half == 1:
                        if m + q + AHEAD < C_PIECES:
                            if kind == "k4":
                                act.wait_ge(lin_done, c_base(i) + step)
                            c_split(i, m + q + AHEAD)
                    for what, s in side:
                        if what == "att":
                            att_scalar_turned(i, s)
                        elif what == "vtc":
                            act.wait_ge(vtc_full, i + 1)
                            act.activation(vtc[:, :, :], aux2[:, 0, :].rearrange("p (c d) -> p c d", c=CH),
                                           ACT.Copy).then_inc(vtc_ready, 1)
                        elif what == "mix":
                            act.wait_ge(yg_step, 1 + 12 * i + 3 * s + 3)
                            act.activation(ygh[:, s, :], xn[s % 2][:, 0:SEQ], ACT.Copy).then_inc(yghi_ready, 1)
                    if stage == "vg" and q == 3:
                        act.wait_ge(vgn, 22 * i + 10)
                        act.activation(vgr[:, :], vgr[:, :], ACT.Sqrt).then_inc(vgr_ready, 1)
                    if stage == "brg":
                        act.wait_ge(m_ready, 8 * i + index + 1)
                        act.activation(mhi[:, index, :], gac[:, n, :], ACT.Copy).then_inc(mhi_ready, 1)
                for k in range(KT):
                    act.wait_ge(xc_ready, 8 * i + k + 1)
                    if k >= 2:
                        act.wait_ge(sq_used, 24 + 8 * i + k - 1)
                    act.activation(sq[k % 2][:, 0:SEQ], h[:, k, META:T], ACT.Square).then_inc(sq_ready, 1)
                act.wait_ge(ms_ready, 6 + 2 * i + 2)
                act.activation(rstd[:, 0:SEQ], rstd[:, 0:SEQ], ACT.Sqrt).then_inc(rstd_ready, 1)
                for k in range(KT):
                    act.wait_ge(xn_ready, 24 + 8 * i + k + 1)
                    act.activation(xhi[:, k, META:T], h[:, k, META:T], ACT.Copy).then_inc(xhi_ready, 1)

            for c in range(CH):
                act.wait_ge(ot_full, c + 1)
                if c >= 2:
                    act.wait_ge(out_sent[c % 2], 16 * (c // 2))
                act.activation(outt[:, c % 2, 0:512], acc[c % 2][:, 0, :], ACT.Copy).then_inc(ot_ready, 1)
                act.activation(outt[:, c % 2, 512:1024], acc[c % 2][:, 1, :], ACT.Copy).then_inc(ot_ready, 1)

        @block.vector
        def _(dve):
            for counted in (og_ready, hm_ready, asc_ready, ya_ready, yg_step, k_ready, win_step):
                dve.sem_inc(counted, 1)
            dve.memset(lbt[:, 7, :], 0.0).then_inc(lo_ready, CREDIT)
            dve.wait_ge(vec_full, 1)
            dve.tensor_copy(vec1[:, :], aux2[:, 0, 0:N_V1]).then_inc(vec_ready, 1)
            dve.wait_ge(vec_full, 2)
            dve.tensor_copy(vec2[:, :], aux2[:, 1, 0:N_V2]).then_inc(vec_ready, 1)
            dve.wait_ge(vec_ready, 2)
            for l in range(DEPTH):
                dve.tensor_scalar(qbias[:, 4 * l:4 * l + 4], vec2[:, NIN2 * l:NIN2 * l + 4], ATT_SCALE, None,
                                  ALU.mult).then_inc(vec_ready, 1)
            l0, l1 = vec1[:, LBA:LBA + NH], vec1[:, LBB:LBB + NH]
            dve.tensor_tensor(lbt[:, 0, :], l0, l1, ALU.max).then_inc(lb_step, 1)
            dve.wait_ge(lb_step, 1)
            dve.tensor_tensor(lbt[:, 1, :], l0, lbt[:, 0, :], ALU.subtract).then_inc(lb_step, 1)
            dve.tensor_tensor(lbt[:, 2, :], l1, lbt[:, 0, :], ALU.subtract).then_inc(lb_step, 1)
            dve.wait_ge(lb_exp, 1)
            dve.tensor_tensor(lbt[:, 5, :], lbt[:, 3, :], lbt[:, 4, :], ALU.add).then_inc(lb_step, 1)
            dve.wait_ge(lb_step, 4)
            dve.reciprocal(lbt[:, 6, :], lbt[:, 5, :]).then_inc(lb_step, 1)
            dve.wait_ge(lb_step, 5)
            dve.tensor_tensor(lbt[:, 0, :], lbt[:, 3, :], lbt[:, 6, :], ALU.mult).then_inc(lb_step, 1)
            dve.tensor_tensor(lbt[:, 1, :], lbt[:, 4, :], lbt[:, 6, :], ALU.mult).then_inc(lb_step, 1)
            dve.wait_ge(lb_step, 7)
            dve.tensor_tensor(lbt[:, 2, :], lbt[:, 0, :], lbt[:, 1, :], ALU.add).then_inc(lb_step, 1)
            dve.wait_ge(lb_step, 8)
            dve.tensor_tensor(lb[:, :], lbt[:, 2, :], lbt[:, 0, :], ALU.subtract).then_inc(lb_step, 1)
            dve.wait_ge(lb_step, 9)
            dve.tensor_scalar(oml[:, :], lb[:, :], -1.0, 1.0, ALU.mult, ALU.add).then_inc(lb_step, 1)

            norm_vector(dve, 0, T, NW0)
            for m in range(AHEAD):
                split_lo(dve, "k8", m, PA)

            def u_lo(G, n):
                dve.wait_ge(uhi_ready, 4 * G + n + 1)
                dve.tensor_tensor(ulo[:, n, :], pu[n % 2][:, :], uhi[:, n, :], ALU.subtract)\
                   .then_inc(ulo_ready, 1)

            A_KINDS = (["k8"] * 8 + ["k4"] * 6) * 2 + ["k8"] * AHEAD
            with dve.Fori(0, A_ITERS) as i:
                for u, (gg, stage, n, kind, m, half) in enumerate(A_PLAN):
                    G, slot = 2 * i + gg, u % 2
                    done = UA // 2 + (A_UNITS // 2) * i + u // 2 + 1
                    if stage == "v":
                        dve.wait_ge(acc_done[slot], done)
                        v, w0 = vpad[slot], 24 * G + 6 * n

                        def coef(j):
                            return pool_c[:, bass.ds(G, 1), j:j + 1].rearrange("p g c -> p (g c)")

                        def shifted(buf, by):
                            return buf[:, META - by:META - by + T]

                        if n:
                            dve.wait_ge(win_step, 1 + w0)
                        dve.tensor_tensor(shifted(spad[0], 0), shifted(v, 1), shifted(v, 0), ALU.add)\
                           .then_inc(win_step, 1)
                        for j, by in enumerate((2, 4, 8)):
                            dve.wait_ge(win_step, 1 + w0 + j + 1)
                            src, dst = spad[j % 2], spad[1 - j % 2]
                            dve.scalar_tensor_tensor(out=shifted(dst, 0), in0=shifted(src, by), scalar=coef(j),
                                                     in1=shifted(src, 0), op0=ALU.mult, op1=ALU.add)\
                               .then_inc(win_step, 1)
                        dve.wait_ge(win_step, 1 + w0 + 4)
                        dve.tensor_tensor(spad[1][:, META:2 * META], spad[1][:, META:2 * META],
                                          pool_c[:, bass.ds(G, 1), 4:20].rearrange("p g c -> p (g c)"),
                                          ALU.mult).then_inc(win_step, 1)
                        dve.wait_ge(win_step, 1 + w0 + 5)
                        if n >= 2:
                            dve.wait_ge(ulo_ready, 4 * G + n - 1)
                        dve.scalar_tensor_tensor(out=pu[slot][:, :], in0=shifted(spad[1], 0), scalar=coef(3),
                                                 in1=shifted(v, 0), op0=ALU.mult, op1=ALU.subtract)\
                           .then_inc(win_step, 1)
                    elif stage == "gate":
                        dve.wait_ge(siga_ready, 4 * G + n + 1)
                        dve.tensor_tensor(halves(ga[:, n, :]), acc_all(slot), halves(sga[slot][:, :]),
                                          ALU.mult).then_inc(acc_done[slot], 1)
                    elif stage == "grp":
                        dve.wait_ge(lin_done, UA + A_UNITS * i + u + 1)
                        if n >= 2:
                            dve.wait_ge(zalo_ready, 4 * G + n - 1)
                        dve.scalar_tensor_tensor(out=halves(pz[slot][:, :]), in0=acc_all(slot),
                                                 scalar=vec1[:, bass.ds(PSC + GT * G + n, 1)],
                                                 in1=halves(ga[:, n, :]), op0=ALU.mult, op1=ALU.mult)\
                           .then_inc(acc_done[slot], 1)
                    else:
                        dve.wait_ge(lin_done, UA + A_UNITS * i + u + 1)
                        dve.tensor_tensor(halves(h[:, n, :]), acc_all(slot), halves(h[:, n, :]), ALU.add)\
                           .then_inc(acc_done[slot], 1)
                    if kind == "k8" or half == 1:
                        split_lo(dve, A_KINDS[m + AHEAD], m + AHEAD, PA + A_PIECES * i)
                    if stage == "v" and n or stage == "gate" and n == 0:
                        u_lo(G, (n - 1) % 4)
                    if stage == "grp":
                        dve.wait_ge(zahi_ready, 4 * G + n + 1)
                        dve.tensor_tensor(zloa[:, n, :], pz[slot][:, :], zhia[:, n, :], ALU.subtract)\
                           .then_inc(zalo_ready, 1)
            norm_vector(dve, 1, T, NW1)

            def b_pair(i, part, process, after):
                pair, u0, p0 = pair_units(i, part)
                par = int(part == "odd")
                slot = 0

                def side():
                    nonlocal slot
                    if process is not None and 1 <= slot <= STEPS:
                        b_vector_step(dve, slot - 1, *process, None)
                    slot += 1

                for j, (what, x) in enumerate(PAIR_UNITS):
                    side()
                    col = bass.ds(2 * pair + x, 1)
                    if what == "f":
                        dve.wait_ge(sgb_ready, 6 * pair + x + 1)
                        dve.tensor_scalar(fb[par][x][:, :], sgb[x][:, :], oml[:, col], lb[:, col],
                                          ALU.mult, ALU.add).then_inc(f_ready, 1)
                        dve.wait_ge(acc_done[x], pair_half(part, i) + j // 2 + 1)
                        dve.tensor_scalar(kb[par][x][:, :], snb[x][:, :], oml[:, col], None, ALU.mult)\
                           .then_inc(k_ready, 1)
                    elif what in "qg":
                        dve.wait_ge(sgb_ready, 6 * pair + (3 if what == "q" else 5) + x)
                        dst = (qb if what == "q" else gb)[par][x]
                        dve.tensor_tensor(dst[:, :], acc[x][:, 0, :], sgb[x][:, 0:SEQ], ALU.mult)\
                           .then_inc(acc_done[x], 1)
                    m = j + AHEAD
                    split_lo_at(p0, m, "k8" if m < 8 else after)
                    side()

            def split_lo_at(p0, m, kind):
                dve.wait_ge(hi_ready, p0 + m + 1)
                dve.tensor_tensor(piece(wlo, kind, m), raw_view(kind, m), piece(whi, kind, m),
                                  ALU.subtract).then_inc(lo_ready, 1)

            def pair_half(part, i):
                if part == "first":
                    return UB // 2
                return UB // 2 + (4 if part == "odd" else 8) + (B_STEPS // 2) * i

            def b_out(u0, p0, ahead):
                for n in range(OUT_UNITS):
                    dve.wait_ge(lin_done, u0 + n + 1)
                    dve.tensor_tensor(h[:, n, META:T], acc[n % 2][:, 0, :], h[:, n, META:T], ALU.add)\
                       .then_inc(acc_done[n % 2], 1)
                    m = n // 2 + AHEAD
                    if n % 2 and (m < 4 or ahead):
                        split_lo_at(p0, m, "k4" if m < 4 else "k8")

            b_pair(None, "first", None, "k8")
            dve.wait_ge(mask_landed, 16)
            dve.wait_ge(a_zero, 2)
            with dve.Fori(0, NG - 1) as i:
                b_pair(i, "odd", (2 * i, 0), "k8")
                b_pair(i, "even", (2 * i + 1, 1), "k4")
                b_out(UB + 24 + B_STEPS * i, PB + 24 + B_PIECES * i, True)
            b_pair(NG - 1, "odd", (2 * (NG - 1), 0), "k4")
            for s in range(STEPS):
                b_vector_step(dve, s, 2 * NG - 1, 1, None)
            b_out(UB + 16 + B_STEPS * (NG - 1), PB + 16 + B_PIECES * (NG - 1), False)
            norm_vector(dve, 2, SEQ, FNW, final=True)

            def att_vector(i, s):
                base = 16 * i
                if s < len(ATT):
                    p, b = ATT[s]
                    lo, z = (0 if b else P), s % 2
                    dve.wait_ge(asc_full, base + s + 1)
                    for x in range(2):
                        dve.scalar_tensor_tensor(out=sc[z][:, x, lo:], in0=nd[:, lo:], scalar=SLOPES[2 * p + x],
                                                 in1=aux[:, 0, 2 * P * x + lo:2 * P * (x + 1)],
                                                 op0=ALU.mult, op1=ALU.add).then_inc(asc_ready, 1)
                    dve.wait_ge(asc_ready, 1 + 2 * (base + s) + 2)
                    dve.tensor_reduce(sm[z][:, 0, :], sc[z][:, :, lo:], AX_X, ALU.max).then_inc(arow, 1)
                    dve.wait_ge(arow, 4 * (base + s) + 1)
                    sink = sinks[:, 2 * p:2 * p + 2]
                    dve.tensor_tensor(sm[z][:, 1, :], sm[z][:, 0, :], sink, ALU.max).then_inc(arow, 1)
                    dve.wait_ge(arow, 4 * (base + s) + 2)
                    dve.tensor_scalar(sm[z][:, 2, :], sm[z][:, 1, :], -1.0, None, ALU.mult).then_inc(arow, 1)
                    dve.tensor_tensor(sm[z][:, 3, :], sink, sm[z][:, 1, :], ALU.subtract).then_inc(arow, 1)

            def att_vector_norm(i, s):
                base = 16 * i
                if s < len(ATT):
                    p, b = ATT[s]
                    lo, z = (0 if b else P), s % 2
                    dve.wait_ge(aexp, 3 * (base + s) + 3)
                    dve.tensor_tensor(sm[z][:, 6, :], sm[z][:, 4, :], sm[z][:, 5, :], ALU.add).then_inc(aprob, 1)
                    dve.wait_ge(aprob, 4 * (base + s) + 1)
                    dve.reciprocal(sm[z][:, 7, :], sm[z][:, 6, :]).then_inc(aprob, 1)
                    dve.wait_ge(aprob, 4 * (base + s) + 2)
                    for x in range(2):
                        dve.tensor_scalar(pr[z][:, x, lo:], pr[z][:, x, lo:], sm[z][:, 7, x:x + 1], None,
                                          ALU.mult).then_inc(aprob, 1)
                if s >= 2 and ATT[s - 2][1] == CH - 1:
                    p = ATT[s - 2][0]
                    dve.wait_ge(ao_full, base + s - 1)
                    dve.tensor_tensor(sq[p % 2][:, 0:SEQ], aux2[:, 1, :], za[:, p, :], ALU.mult)\
                       .then_inc(ya_ready, 1)
                    dve.wait_ge(yahi_ready, 4 * i + p + 1)
                    dve.tensor_tensor(yal[:, p, :], sq[p % 2][:, 0:SEQ], yah[:, p, :], ALU.subtract)\
                       .then_inc(yalo_ready, 1)

            def mix_vector(i, g):
                y, w0 = xn[g % 2][:, 0:SEQ], 12 * i + 3 * g
                dve.wait_ge(mix_full, 4 * i + g + 1)
                dve.tensor_tensor(y.rearrange("p (c t) -> p c t", c=CH),
                                  aux[:, 1, :].rearrange("p (c t) -> p c t", c=CH),
                                  bsp[:, g:g + 1, :].to_broadcast([P, CH, P]), ALU.add).then_inc(yg_step, 1)
                dve.wait_ge(yg_step, 1 + w0 + 1)
                dve.tensor_tensor(y, y, ug[:, g, :], ALU.mult).then_inc(yg_step, 1)
                dve.wait_ge(yg_step, 1 + w0 + 2)
                dve.tensor_tensor(y, y, zg[:, g, :], ALU.mult).then_inc(yg_step, 1)
                dve.wait_ge(yghi_ready, 4 * i + g + 1)
                dve.tensor_tensor(ygl[:, g, :], y, ygh[:, g, :], ALU.subtract).then_inc(yglo_ready, 1)

            def vg_norm(i):
                w0 = 22 * i
                for c in range(CH):
                    dve.wait_ge(vgg_ready, 4 * i + c + 1)
                    dve.bn_stats(vgst[:, c, 0:6], vn[:, c, :]).then_inc(vgn, 1)
                for c in range(CH):
                    wait_apart(dve, "dve", (vgn, w0 + 4 + c))
                    dve.bn_aggr(vgst[:, c, 6:8], vgst[:, c, 0:6]).then_inc(vgn, 1)
                dve.wait_ge(vgn, w0 + 8)
                dve.tensor_scalar(vgr[:, :], vgst[:, :, 7], LN_EPS, None, ALU.add).then_inc(vgn, 1)
                dve.wait_ge(vgn, w0 + 9)
                dve.reciprocal(vgr[:, :], vgr[:, :]).then_inc(vgn, 1)
                dve.wait_ge(vgr_ready, i + 1)
                for c in range(CH):
                    v = vn[:, c, :]
                    dve.tensor_scalar(v, v, vgst[:, c, 6:7], vgr[:, c:c + 1], ALU.subtract, ALU.mult)\
                       .then_inc(vgn, 1)
                    dve.wait_ge(vgn, w0 + 11 + 3 * c)
                    dve.tensor_tensor(v, v, gvg[:, :], ALU.mult).then_inc(vgn, 1)
                    dve.wait_ge(vgn, w0 + 12 + 3 * c)
                    dve.tensor_tensor(v, v, bevg[:, :], ALU.add).then_inc(vgn, 1)

            def c_split(i, m):
                split_lo(dve, C_KIND[m], m, PC + C_PIECES * i)

            dve.wait_ge(c_landed, 32)
            with dve.Fori(0, DEPTH) as i:
                for m in range(AHEAD):
                    c_split(i, m)
                for (stage, index, kind, m, half, u), q, side in C_ORDER:
                    slot, n = u % 2, index % 4
                    psum = acc[slot][:, 0, :]
                    step = c_base(i) + STEP_OF[stage, index]
                    if stage in ("za", "zg"):
                        dve.wait_ge(sigc_ready, 8 * i + (4 if stage == "zg" else 0) + n + 1)
                        dve.scalar_tensor_tensor(out=(za if stage == "za" else zg)[:, n, :], in0=psum,
                                                 scalar=vec2[:, bass.ds(NIN2 * i + COL2[stage] + n, 1)],
                                                 in1=sgc[slot][:, :], op0=ALU.add, op1=ALU.mult)\
                           .then_inc(acc_done[slot], 1)
                    elif stage == "vg" and q == 3:
                        dve.wait_ge(lin_done, step)
                        dve.wait_ge(lc_landed, 96 * i + 96)
                        for c in range(CH):
                            dve.tensor_tensor(vn[:, c, :], acc[c // 2][:, c % 2, :], bvg[:, :], ALU.add)\
                               .then_inc(acc_done[c // 2] if c % 2 else vgb_ready, 1)
                    elif stage == "bra":
                        dve.wait_ge(lin_done, step)
                        dve.tensor_tensor(gac[:, n, :], psum, gac[:, n, :], ALU.mult).then_inc(acc_done[slot], 1)
                    elif stage == "brg":
                        dve.wait_ge(lin_done, step)
                        dve.tensor_tensor(ggc[:, n, :], psum, ggc[:, n, :], ALU.mult).then_inc(acc_done[slot], 1)
                        dve.wait_ge(acc_done[slot], c_done(i, u))
                        dve.tensor_tensor(gac[:, n, :], gac[:, n, :], ggc[:, n, :], ALU.add)\
                           .then_inc(m_ready, 1)
                    elif stage == "wo":
                        dve.wait_ge(acc_done[slot], c_done(i, u))
                        dve.scalar_tensor_tensor(out=h[:, index, META:T], in0=h[:, index, META:T],
                                                 scalar=ALPHA, in1=xn[slot][:, 0:SEQ], op0=ALU.mult,
                                                 op1=ALU.add).then_inc(wo_ready, 1)
                    for what, s in side:
                        if what == "att":
                            att_vector(i, s)
                    if (kind != "k4" or half == 1) and m + q + AHEAD < C_PIECES:
                        c_split(i, m + q + AHEAD)
                    for what, s in side:
                        if what == "att":
                            att_vector_norm(i, s)
                        elif what == "ws":
                            dve.wait_ge(ws_full, i + 1)
                            dve.tensor_tensor(wst[:, :, :], aux2[:, 1, :].rearrange("p (g t) -> p g t", g=4),
                                              causal[:, None, :].to_broadcast([P, 4, P]), ALU.mult)\
                               .then_inc(ws_ready, 1)
                        elif what == "mix":
                            mix_vector(i, s)
                    if stage == "vg" and q == 3:
                        vg_norm(i)
                    if stage == "brg":
                        dve.wait_ge(mhi_ready, 8 * i + index + 1)
                        dve.tensor_tensor(mlo[:, index, :], gac[:, n, :], mhi[:, index, :], ALU.subtract)\
                           .then_inc(mlo_ready, 1)
                dve.wait_ge(mean_used, 8 * i + 8)
                for k in range(KT):
                    dve.tensor_tensor(h[:, k, META:T], h[:, k, META:T], aux[:, 1, :], ALU.subtract)\
                       .then_inc(xc_ready, 1)
                dve.wait_ge(sq_used, 24 + 8 * i + 8)
                inverse_vector(dve, 3 + i, aux[:, 0, :], rstd[:, 0:SEQ], LN_EPS, SEQ)

                def scaled(k):
                    dve.tensor_tensor(h[:, k, META:T], h[:, k, META:T], rstd[:, 0:SEQ], ALU.mult)\
                       .then_inc(ln_t, 1)
                    dve.wait_ge(ln_t, 8 * i + k + 1)
                    dve.tensor_scalar(h[:, k, META:T], h[:, k, META:T], vec2[:, bass.ds(LNG + 8 * i + k, 1)],
                                      vec2[:, bass.ds(LNB + 8 * i + k, 1)], ALU.mult, ALU.add)\
                       .then_inc(xn_ready, 1)

                scaled(0)
                for k in range(KT):
                    if k + 1 < KT:
                        scaled(k + 1)
                    dve.wait_ge(xhi_ready, 24 + 8 * i + k + 1)
                    dve.tensor_tensor(xlo[:, k, META:T], h[:, k, META:T], xhi[:, k, META:T], ALU.subtract)\
                       .then_inc(xlo_ready, 1)


_INS = ["x", "meta_tokens", "norm_w", "pool_w_in", "pool_w_grp", "pool_scale", "pool_w_out", "hgrn_w_in",
        "hgrn_lb_logits", "hgrn_o_norm", "hgrn_w_out", "final_norm_w", "w_in_2", "b_in_2", "attn_sinks_2",
        "gmlp_ln_g_2", "gmlp_ln_b_2", "w_spatial_2", "b_spatial_2", "w_branch_attn_2", "w_branch_gmlp_2",
        "w_out_2", "b_out_2", "ln_g_2", "ln_b_2"]


def shape_constants(np):
    pool = np.zeros((P, NG, 20), np.float32)
    for g, w in enumerate((2, 4, 8, 16)):
        pool[:, g, 0:3] = [w >= 4, w >= 8, w >= 16]
        pool[:, g, 3] = 1.0 / w
        pool[:, g, 4:20] = w / np.minimum(np.arange(16) + 1, w)
    s = np.arange(P)[:, None]
    masks = [s == np.arange(P)[None, :]]
    for level in range(LEVELS):
        m = 2 ** level
        t = np.array([t for t in range(P) if t & m])[None, :]
        masks.append((s // (2 * m) == t // (2 * m)) & (s & m == 0))
    dist = np.arange(P)[:, None] + P - np.arange(2 * P)[None, :]
    nd = np.where((dist >= 0) & (dist < P), -dist, -1e30)
    return {"c_ident": np.eye(P, dtype=np.float32), "c_pool": pool,
            "c_masks": np.concatenate(masks, 1).astype(np.int32), "c_nd": nd.astype(np.float32),
            "c_causal": (s <= np.arange(P)[None, :]).astype(np.float32)}


def kernel(**inputs):
    import numpy as np
    import concourse.bacc as bacc
    from concourse import mybir as _mybir
    from concourse.bass_utils import run_bass_kernel_spmd as run

    nc = bacc.Bacc("TRN2", target_bir_lowering=False, num_devices=1)
    arrays, args = {}, {}
    for name, value in [(n, inputs[n]) for n in _INS] + list(shape_constants(np).items()):
        x = np.ascontiguousarray(value)
        arrays[f"in_{name}"] = x
        args[name] = nc.dram_tensor(f"in_{name}", x.shape, _mybir.dt.from_np(x.dtype), kind="ExternalInput").ap()
    out = nc.dram_tensor("out_0", (1, SEQ, D), F32, kind="ExternalOutput").ap()
    program(nc, args, out)
    r = run(nc, [arrays], core_ids=[0])
    return r.results[0]["out_0"]
```

```python
from contextlib import ExitStack

import concourse.bass as bass
from concourse import mybir

F32 = mybir.dt.float32
F32R = mybir.dt.float32r
I32 = mybir.dt.int32
ALU = mybir.AluOpType
ACT = mybir.ActivationFunctionType
AX_X = mybir.AxisListType.X

P = 128
D = 1024
KT = D // P
META = 16
SEQ = 512
T = META + SEQ
TH = T // 2
NG = 4
GT = 4
E = 2048
NH = E // P
CH = SEQ // P
LEVELS = 7
MASKED = 5
EPS = 1e-6
LN_EPS = 1e-5
DEPTH = 2
IN2 = 4864
HD = 64
ATT_SCALE = HD ** -0.5
SLOPES = [2.0 ** -(n + 1) for n in range(8)]
ALPHA = (2 * DEPTH) ** 0.25
RAW = 2
PIECES = 4
AHEAD = 3
CREDIT = 2

COL2 = {"q": 0, "k": 4, "v": 5, "za": 6, "u": 10, "vg": 14, "zg": 18, "ga": 22, "gg": 30}
NIN2 = IN2 // P

NW0, NW1, FNW, PSC, ONW, LBA, LBB, N_V1 = 0, 8, 16, 24, 40, 56, 72, 88
BIN, BOUT, LNG, LNB, N_V2 = 0, 76, 92, 108, 124


def plan_a():
    units = []
    for gg in range(2):
        m = 14 * gg
        units += [(gg, "v", n, "k8", m + n, 0) for n in range(4)]
        units += [(gg, "gate", n, "k8", m + 4 + n, 0) for n in range(4)]
        units += [(gg, "grp", n, "k4", m + 8 + n // 2, n % 2) for n in range(4)]
        units += [(gg, "out", n, "k4", m + 10 + n // 2, n % 2) for n in range(8)]
    return units


def plan_c():
    units, m, u = [], 0, 0

    def add(stage, first, count, kind):
        nonlocal m, u
        for n in range(count):
            half = n % 2 if kind == "k4" else 0
            units.append((stage, first + n, kind, m, half, u))
            m += {"k8": 1, "k4": n % 2, "vg": 4}[kind]
            u += 2 if kind == "vg" else 1

    for stage, count in (("q", 4), ("k", 1), ("v", 1), ("za", 4), ("u", 4)):
        add(stage, 0, count, "k8")
    add("vg", 0, 1, "vg")
    add("zg", 0, 4, "k8")
    for half in range(2):
        add("ga", 4 * half, 4, "k8")
        add("gg", 4 * half, 4, "k8")
        add("bra", 4 * half, 4, "k4")
        add("brg", 4 * half, 4, "k4")
    add("wo", 0, 8, "k8")
    return units, m, u


A_PLAN = plan_a()
C_PLAN, C_PIECES, C_UNITS = plan_c()
A_ITERS, A_PIECES, A_UNITS = 2, 28, len(A_PLAN)
PAIR_UNITS = [("f", 0), ("f", 1), ("q", 0), ("q", 1), ("i", 0), ("i", 1), ("g", 0), ("g", 1)]
OUT_UNITS = 8
C_STEPS = C_UNITS + 2

PA, UA = 0, KT
PB, UB = PA + A_ITERS * A_PIECES, UA + A_ITERS * A_UNITS
B_PIECES, B_STEPS = 20, 24
PC, UC = PB + NG * B_PIECES, UB + NG * B_STEPS


def program(nc, a, out):
    with ExitStack() as ctx:
        def sb(name, shape, dt=F32, where=ctx):
            return where.enter_context(nc.sbuf_tensor(name, shape, dt))

        def sem(name):
            return ctx.enter_context(nc.semaphore(name))

        acc = [ctx.enter_context(nc.psum_tensor(f"acc{s}", [P, 2, 512], F32)) for s in range(2)]
        aux = ctx.enter_context(nc.psum_tensor("aux", [P, 2, 512], F32))
        aux2 = ctx.enter_context(nc.psum_tensor("aux2", [P, 2, 512], F32))

        h = sb("h", [P, KT, T])
        xhi = sb("xhi", [P, KT, T], F32R)
        xlo = sb("xlo", [P, KT, T], F32R)
        raw = [sb(f"raw{s}", [P, 2048]) for s in range(RAW)]
        whi = [sb(f"whi{s}", [P, 1024], F32R) for s in range(PIECES)]
        wlo = [sb(f"wlo{s}", [P, 1024], F32R) for s in range(PIECES)]
        ident = sb("ident", [P, P])
        vec1 = sb("vec1", [P, N_V1])
        vec2 = sb("vec2", [P, N_V2])
        ones_d = sb("ones_d", [P, P])
        sq = [sb(f"sq{s}", [P, T]) for s in range(2)]
        rstd = sb("rstd", [P, T])
        xn = [sb(f"xn{s}", [P, T]) for s in range(2)]
        lb = sb("lb", [P, NH])
        oml = sb("oml", [P, NH])
        qbias = sb("qbias", [P, DEPTH * 4])

        with ExitStack() as in_a:
            xt = sb("xt", [P, CH, D], where=in_a)
            mt = sb("mt", [META, D], where=in_a)
            rows1 = sb("rows1", [N_V1, P], where=in_a)
            rows2 = sb("rows2", [N_V2, P], where=in_a)
            lbt = sb("lbt", [P, 8, NH], where=in_a)
            vpad = [sb(f"vpad{s}", [P, META + T], where=in_a) for s in range(2)]
            spad = [sb(f"spad{s}", [P, META + T], where=in_a) for s in range(2)]
            pu = [sb(f"pu{s}", [P, T], where=in_a) for s in range(2)]
            uhi = sb("uhi", [P, GT, T], F32R, where=in_a)
            ulo = sb("ulo", [P, GT, T], F32R, where=in_a)
            sga = [sb(f"sga{s}", [P, T], where=in_a) for s in range(2)]
            ga = sb("ga", [P, GT, T], where=in_a)
            pz = [sb(f"pz{s}", [P, T], where=in_a) for s in range(2)]
            zhia = sb("zhia", [P, GT, T], F32R, where=in_a)
            zloa = sb("zloa", [P, GT, T], F32R, where=in_a)
            pool_c = sb("pool_c", [P, NG, 20], where=in_a)

        with ExitStack() as in_b:
            def heads(name, shape):
                return [[sb(f"{name}{p}{x}", shape, where=in_b) for x in range(2)] for p in range(2)]

            fb = heads("fb", [P, T])
            kb = heads("kb", [P, T])
            qb = heads("qb", [P, SEQ])
            ib = heads("ib", [P, T])
            gb = heads("gb", [P, SEQ])
            tb = [{m: sb(f"tb{m}_{x}", [P, T // m if m <= META else SEQ // m], where=in_b)
                   for m in (2, 4, 8, 16, 32, 64, 128)} for x in range(2)]
            sgb = [sb(f"sgb{x}", [P, T], where=in_b) for x in range(2)]
            snb = [sb(f"snb{x}", [P, T], where=in_b) for x in range(2)]
            ab = [sb(f"ab{x}", [P, CH, P], where=in_b) for x in range(2)]
            vt = [sb(f"vt{x}", [P, CH, P], where=in_b) for x in range(2)]
            vtm = [sb(f"vtm{x}", [META, P], where=in_b) for x in range(2)]
            kt = [sb(f"kt{x}", [P, CH - 1, P], where=in_b) for x in range(2)]
            ktm = [sb(f"ktm{x}", [META, P], where=in_b) for x in range(2)]
            st = [sb(f"st{x}", [P, CH, P], where=in_b) for x in range(2)]
            og = [sb(f"og{x}", [P, SEQ], where=in_b) for x in range(2)]
            zhib = sb("zhib", [P, GT, SEQ], F32R, where=in_b)
            zlob = sb("zlob", [P, GT, SEQ], F32R, where=in_b)
            om = sb("om", [P, 32], where=in_b)
            masks = sb("masks", [P, P + 64 * MASKED], I32, where=in_b)

        in_c = ExitStack()
        nd = sb("nd", [P, 2 * P], where=in_c)
        bvg = sb("bvg", [P, 512], where=in_c)
        gvg = sb("gvg", [P, 512], where=in_c)
        bevg = sb("bevg", [P, 512], where=in_c)
        bsp = sb("bsp", [P, 4, P], where=in_c)
        sinks = sb("sinks", [P, 8], where=in_c)
        wst = sb("wst", [P, 4, P], where=in_c)
        causal = sb("causal", [P, P], where=in_c)
        sm = [sb(f"sm{s}", [P, 8, 2], where=in_c) for s in range(2)]
        vgst = sb("vgst", [P, CH, 8], where=in_c)
        vgr = sb("vgr", [P, CH], where=in_c)
        gac = sb("gac", [P, 4, SEQ], where=in_c)
        ggc = sb("ggc", [P, 4, SEQ], where=in_c)
        with ExitStack() as made_from:
            qc = sb("qc", [P, 4, SEQ], where=made_from)
            za = sb("za", [P, 4, SEQ], where=made_from)
            ug = sb("ug", [P, 4, SEQ], where=made_from)
            zg = sb("zg", [P, 4, SEQ], where=made_from)
        yah = sb("yah", [P, 4, SEQ], F32R, where=in_c)
        yal = sb("yal", [P, 4, SEQ], F32R, where=in_c)
        ygh = sb("ygh", [P, 4, SEQ], F32R, where=in_c)
        ygl = sb("ygl", [P, 4, SEQ], F32R, where=in_c)
        with ExitStack() as before_m:
            kf = sb("kf", [P, SEQ], where=before_m)
            kc = [sb(f"kc{n}", [P, 2, SEQ], where=before_m) for n in range(2)]
            vf = sb("vf", [P, SEQ], where=before_m)
            vtc = sb("vtc", [P, CH, P], where=before_m)
            vn = sb("vn", [P, CH, 512], where=before_m)
            sc = [sb(f"sc{s}", [P, 2, 2 * P], where=before_m) for s in range(2)]
            pr = [sb(f"pr{s}", [P, 2, 2 * P], where=before_m) for s in range(2)]
            pt = [sb(f"pt{s}", [P, 4, P], where=before_m) for s in range(2)]
            sgc = [sb("sgc0", [P, SEQ], where=before_m), rstd[:, 0:SEQ]]
        with ExitStack() as after_m:
            mhi = sb("mhi", [P, KT, SEQ], F32R, where=after_m)
            mlo = sb("mlo", [P, KT, SEQ], F32R, where=after_m)
        in_c.close()
        outt = gac[:, :, :].rearrange("p (s n) t -> p s (n t)", s=2)
        ws = gac[:, 0, :].rearrange("p (g s) -> p g s", g=4)

        raw_landed = [sem(f"raw_landed{s}") for s in range(RAW)]
        hi_ready, lo_ready, lin_done = sem("hi_ready"), sem("lo_ready"), sem("lin_done")
        acc_done = [sem(f"acc_done{s}") for s in range(2)]
        const_landed, x_landed = sem("const_landed"), sem("x_landed")
        c_landed, mask_landed = sem("c_landed"), sem("mask_landed")
        ones_ready, pads_ready = sem("ones_ready"), sem("pads_ready")
        vec_full, vec_ready = sem("vec_full"), sem("vec_ready")
        lb_step, lb_exp = sem("lb_step"), sem("lb_exp")
        sq_ready, sq_used, ms_ready = sem("sq_ready"), sem("sq_used"), sem("ms_ready")
        rstd_ready, xn_ready = sem("rstd_ready"), sem("xn_ready")
        xhi_ready, xlo_ready, xlo_pool = sem("xhi_ready"), sem("xlo_ready"), sem("xlo_pool")
        win_step = sem("win_step")
        uhi_ready, ulo_ready = sem("uhi_ready"), sem("ulo_ready")
        siga_ready, ga_ready = sem("siga_ready"), sem("ga_ready")
        zahi_ready, zalo_ready = sem("zahi_ready"), sem("zalo_ready")
        a_zero = sem("a_zero")
        sgb_ready, f_ready, k_ready = sem("sgb_ready"), sem("f_ready"), sem("k_ready")
        snb_ready, qg_ready = sem("snb_ready"), sem("qg_ready")
        vt_full, vt_ready = sem("vt_full"), sem("vt_ready")
        sc_full, sc_done, q_step, k_step = sem("sc_full"), sem("sc_done"), sem("q_step"), sem("k_step")
        kt_full, kt_ready = sem("kt_full"), sem("kt_ready")
        kv_full, st_ready = sem("kv_full"), sem("st_ready")
        o_full, o2_ready, on_ready = sem("o_full"), sem("o2_ready"), sem("on_ready")
        ot_turned, hm_ready, hr_ready = sem("ot_turned"), sem("hm_ready"), sem("hr_ready")
        zb_ready, zbhi_ready, zblo_ready = sem("zb_ready"), sem("zbhi_ready"), sem("zblo_ready")
        lc_landed, ws_full, ws_ready = sem("lc_landed"), sem("ws_full"), sem("ws_ready")
        sigc_ready, kd_landed = sem("sigc_ready"), sem("kd_landed")
        kz_ready, vn_step = sem("kz_ready"), sem("vn_step")
        vtc_full, vtc_ready = sem("vtc_full"), sem("vtc_ready")
        asc_full, asc_ready, arow = sem("asc_full"), sem("asc_ready"), sem("arow")
        aexp, aprob = sem("aexp"), sem("aprob")
        apt_full, apt_ready, ao_full = sem("apt_full"), sem("apt_ready"), sem("ao_full")
        ya_ready, yahi_ready, yalo_ready = sem("ya_ready"), sem("yahi_ready"), sem("yalo_ready")
        vgb_ready, vgg_ready, vgn, vgr_ready = (sem("vgb_ready"), sem("vgg_ready"), sem("vgn"),
                                                sem("vgr_ready"))
        mix_full, yg_step = sem("mix_full"), sem("yg_step")
        yghi_ready, yglo_ready = sem("yghi_ready"), sem("yglo_ready")
        m_ready, mhi_ready, mlo_ready = sem("m_ready"), sem("mhi_ready"), sem("mlo_ready")
        wo_ready, mean_used, xc_ready, ln_t = (sem("wo_ready"), sem("mean_used"), sem("xc_ready"),
                                               sem("ln_t"))
        ot_full, ot_ready, out_sent = sem("ot_full"), sem("ot_ready"), [sem("out_sent0"), sem("out_sent1")]

        passed = {"sp": sem("passed_sp"), "pool": sem("passed_pool"), "dve": sem("passed_dve")}

        def wait_apart(eng, name, *waits):
            for s, v in waits:
                eng.wait_ge(s, v)
            eng.sem_inc(passed[name], 1)

        def raw_view(kind, m):
            slot, q = raw[(m // 2) % RAW], m % 2
            if kind == "vg":
                return slot[:, 1024 * q:1024 * (q + 1)].rearrange("p (k n) -> p k n", k=2)
            w = 128 if kind == "k8" else 256
            return slot[:, :].rearrange("p (k n) -> p k n", n=2 * w)[:, :, q * w:(q + 1) * w]

        def piece(bufs, kind, m):
            return bufs[m % PIECES][:, :].rearrange("p (k n) -> p k n", k={"k8": 8, "k4": 4, "vg": 2}[kind])

        def split_hi(act, kind, m, landed, freed):
            act.wait_ge(raw_landed[(m // 2) % RAW], landed)
            if freed is not None:
                act.wait_ge(lin_done, freed)
            act.activation(piece(whi, kind, m), raw_view(kind, m), ACT.Copy).then_inc(hi_ready, 1)

        def split_lo(dve, kind, m, before):
            dve.wait_ge(hi_ready, before + m + 1)
            dve.tensor_tensor(piece(wlo, kind, m), raw_view(kind, m), piece(whi, kind, m),
                              ALU.subtract).then_inc(lo_ready, 1)

        def products(pe, dst, stat, mov, first, last):
            pe.matmul(dst, stat[0], mov[0], start=first, stop=False)
            pe.matmul(dst, stat[0], mov[1], start=False, stop=False)
            return pe.matmul(dst, stat[1], mov[0], start=False, stop=last)

        def unit(pe, slot, kind, m, half, K, rhs, tokens, k_wait=None, mid=None):
            hi, lo = piece(whi, kind, m), piece(wlo, kind, m)
            cols = slice(128 * half, 128 * half + 128)
            parts = [(0, META, SEQ)] if tokens == SEQ else [(0, 0, TH), (1, TH, TH)]
            for n, (bank, t0, w) in enumerate(parts):
                for k in range(K):
                    if n == 0 and k_wait is not None:
                        k_wait(k)
                    mm = products(pe, acc[slot][:, bank, 0:w], (hi[:, k, cols], lo[:, k, cols]),
                                  rhs(k, t0, w), k == 0, k == K - 1)
                    if mid is not None and k == K // 2 - 1 and tokens == SEQ:
                        mid()
                if mid is not None and n == 0 and tokens == T:
                    mid()
            mm.then_inc(lin_done, 1)

        def of_x(k, t0, w):
            return xhi[:, k, t0:t0 + w], xlo[:, k, t0:t0 + w]

        def acc_all(slot):
            return acc[slot][:, :, 0:TH]

        def halves(ap):
            return ap.rearrange("p (b t) -> p b t", b=2)

        def norm_scalar(act, v, tokens, h_ready):
            for k in range(KT):
                h_ready(act, k)
                square(act, v, k, T - tokens)
            root(act, v, tokens)

        def weighted_hi(act, v, k, wcol):
            act.activation(xhi[:, k, :], h[:, k, :], ACT.Copy, scale=vec1[:, wcol + k:wcol + k + 1])\
               .then_inc(xhi_ready, 1)

        def weighted_lo(dve, v, k, wcol):
            dve.wait_ge(xhi_ready, 8 * v + k + 1)
            dve.scalar_tensor_tensor(out=xlo[:, k, :], in0=h[:, k, :], scalar=vec1[:, wcol + k:wcol + k + 1],
                                     in1=xhi[:, k, :], op0=ALU.mult, op1=ALU.subtract).then_inc(xlo_ready, 1)

        def square(act, v, k, t0):
            if k >= 2:
                act.wait_ge(sq_used, 8 * v + k - 1)
            act.activation(sq[k % 2][:, 0:T - t0], h[:, k, t0:T], ACT.Square).then_inc(sq_ready, 1)

        def root(act, v, tokens):
            act.wait_ge(ms_ready, 2 * v + 2)
            act.activation(rstd[:, 0:tokens], rstd[:, 0:tokens], ACT.Sqrt).then_inc(rstd_ready, 1)

        def weighted_inverse(dve, v):
            dve.wait_ge(sq_used, 8 * v + 8)
            inverse_vector(dve, v, aux[:, :, 0:TH], halves(rstd[:, :]), EPS, T)

        def norm_tensor(pe, v, tokens, tiles=range(KT)):
            parts = [(1, 0, SEQ)] if tokens == SEQ else [(0, 0, TH), (1, TH, TH)]
            for k in tiles:
                pe.wait_ge(sq_ready, 8 * v + k + 1)
                for bank, t0, w in parts:
                    mm = pe.matmul(aux[:, bank, 0:w], ones_d[:, :], sq[k % 2][:, t0:t0 + w],
                                   start=(k == 0), stop=(k == KT - 1))
                mm.then_inc(sq_used, 1)

        def inverse_vector(dve, v, src, dst, eps, tokens):
            dve.tensor_scalar(dst, src, eps, None, ALU.add).then_inc(ms_ready, 1)
            dve.wait_ge(ms_ready, 2 * v + 1)
            dve.reciprocal(rstd[:, 0:tokens], rstd[:, 0:tokens]).then_inc(ms_ready, 1)
            dve.wait_ge(rstd_ready, v + 1)

        def norm_vector(dve, v, tokens, wcol):
            t0 = T - tokens
            dve.wait_ge(sq_used, 8 * v + 8)
            inverse_vector(dve, v, aux[:, 1, :], rstd[:, 0:SEQ], EPS, tokens)

            for k in range(KT):
                dve.scalar_tensor_tensor(out=h[:, k, t0:T], in0=h[:, k, t0:T], scalar=vec1[:, wcol + k:wcol + k + 1],
                                         in1=rstd[:, 0:tokens], op0=ALU.mult, op1=ALU.mult)\
                   .then_inc(xn_ready, 1)

        def x_wait(pe, v):
            return lambda k: pe.wait_ge(xlo_ready, 8 * v + k + 1)

        def q_after(pair, level, x):
            return pair * 2 * (LEVELS + 1) + 2 * level + x + 1

        def k_after(pair, level, x, blocks=False):
            return pair * 4 * LEVELS + 4 * (level - 1) + 2 * x + (2 if blocks else 1)

        def at_level(x, par, m):
            whole = fb[par][x] if m == 1 else tb[x][m]
            n_meta = META // m if m <= META else 0
            n_all = n_meta + SEQ // m
            seq = whole[:, n_meta:n_all].rearrange("p (b two) -> p b two", two=2)
            both = whole[:, 0:n_all].rearrange("p (b two) -> p b two", two=2) if m < META else seq
            return both, seq

        def second_halves(ap, m):
            return ap.rearrange("p (b two m) -> p b two m", two=2, m=m)[:, :, 1, :]

        def first_halves(ap, m):
            return ap.rearrange("p (b two m) -> p b two m", two=2, m=m)[:, :, 0, :]

        def unmasked(level):
            return [(c, n) for c in range(CH) for n in range(64 >> (level - 1))] if level > MASKED else []

        def mask_of(level):
            if level == 0:
                return masks[:, None, 0:P].to_broadcast([P, CH, P])
            m = 2 ** (level - 1)
            cols = masks[:, P + 64 * (level - 1):P + 64 * level].rearrange("p (b m) -> p b m", m=m)
            return cols[:, None, :, :].to_broadcast([P, CH, 64 // m, m])

        STEPS = 6 + LEVELS
        STEP_AT = {s + (1 if s < LEVELS + 5 else 2): s for s in range(STEPS)}

        def b_tensor_step(pe, s, pair, par):
            for x in range(2):
                big, small = aux2[:, x, :], aux[:, x, :]
                if s == 0:
                    pe.wait_ge(on_ready, 1 + 2 * pair)
                    pe.wait_ge(zb_ready, 1 + 2 * pair)
                    for c in range(CH):
                        pe.transpose(big[:, P * c:P * c + P],
                                     ib[par][x][:, META + P * c:META + P * c + P], ident[:, :])
                    pe.transpose(small[0:META, 0:P], ib[par][x][:, 0:META], ident[:, :]).then_inc(vt_full, 1)
                elif s <= LEVELS + 1:
                    level = s - 1
                    if level == 0:
                        pe.wait_ge(k_ready, 1 + 2 * pair + x + 1)
                        pe.wait_ge(qg_ready, 2 + 4 * pair + x + 1)
                        pe.wait_ge(vt_ready, 4 * pair + 2 * x + 2)
                    else:
                        pe.wait_ge(q_step, q_after(pair, level - 1, x))
                        if level > 1:
                            pe.wait_ge(k_step, k_after(pair, level - 1, x))
                        pe.wait_ge(sc_done, 16 * pair + 2 * (level - 1) + x + 1)
                    m = 2 ** (level - 1) if level else None
                    for c, n in unmasked(level):
                        s0, t0 = P * c + 2 * m * n, P * c + 2 * m * n + m
                        mm = pe.matmul(small[2 * m * n:2 * m * n + m, m * c:m * c + m],
                                       kb[par][x][:, META + s0:META + s0 + m], qb[par][x][:, t0:t0 + m],
                                       start=True, stop=True)
                    for c in range(CH if level <= MASKED else 0):
                        keys = kb[par][x][:, META + P * c:META + P * c + P]
                        q = qb[par][x][:, P * c:P * c + P]
                        if level == 0:
                            dst = small[:, P * c:P * c + P]
                        else:
                            q = second_halves(q, m)
                            dst = small[:, 64 * c:64 * c + 64].rearrange("p (b m) -> p b m", m=m)
                        mm = pe.matmul(dst, keys, q, start=True, stop=True)
                    mm.then_inc(sc_full, 1)
                elif s == LEVELS + 2:
                    pe.wait_ge(k_step, k_after(pair, LEVELS, x))
                    pe.wait_ge(sc_done, 16 * pair + 14 + x + 1)
                    for c in range(CH - 1):
                        pe.transpose(big[:, P * c:P * c + P],
                                     kb[par][x][:, META + P * c:META + P * c + P], ident[:, :])
                    pe.transpose(big[0:META, 3 * P:4 * P], kb[par][x][:, 0:META], ident[:, :])\
                      .then_inc(kt_full, 1)
                elif s == LEVELS + 3:
                    pe.wait_ge(kt_ready, 4 * pair + 2 * x + 2)
                    pe.wait_ge(sc_done, 16 * pair + 14 + x + 1)
                    pe.matmul(small[:, 0:P], ktm[x][:, :], vtm[x][:, :], start=True, stop=True)
                    for c in range(CH - 1):
                        mm = pe.matmul(small[:, P * (c + 1):P * (c + 2)], kt[x][:, c, :], vt[x][:, c, :],
                                       start=True, stop=True)
                    mm.then_inc(kv_full, 1)
                elif s == LEVELS + 4:
                    pe.wait_ge(st_ready, 8 * pair + 4 * x + 4)
                    pe.wait_ge(q_step, q_after(pair, LEVELS, x))
                    for c in range(CH):
                        pe.matmul(big[:, P * c:P * c + P], ab[x][:, c, :], vt[x][:, c, :], start=True,
                                  stop=False)
                        mm = pe.matmul(big[:, P * c:P * c + P], qb[par][x][:, P * c:P * c + P],
                                       st[x][:, c, :], start=False, stop=True)
                    mm.then_inc(o_full, 1)
                else:
                    pe.wait_ge(on_ready, 1 + 2 * pair + x + 1)
                    for c in range(CH):
                        mm = pe.transpose(small[:, P * c:P * c + P], xn[x][:, P * c:P * c + P], ident[:, :])
                    mm.then_inc(ot_turned, 1)

        def b_vector_step(dve, s, pair, par):
            if 1 <= s <= LEVELS + 1:
                level = s - 1
                for x in range(2):
                    dve.wait_ge(sc_full, 16 * pair + 2 * level + x + 1)
                    q = qb[par][x][:, :]
                    if level == 0:
                        dve.tensor_tensor(q, q, fb[par][x][:, META:T], ALU.mult).then_inc(q_step, 1)
                        dve.copy_predicated(ab[x][:, :, :], mask_of(0),
                                            aux[:, x, :].rearrange("p (c t) -> p c t", c=CH))\
                           .then_inc(sc_done, 1)
                        continue
                    dve.wait_ge(sc_done, 16 * pair + 2 * (level - 1) + x + 1)
                    dve.wait_ge(q_step, q_after(pair, level - 1, x))
                    if level > 1:
                        dve.wait_ge(k_step, k_after(pair, level - 1, x, True))
                    m = 2 ** (level - 1)
                    nb = 64 // m
                    blocks = at_level(x, par, m)[1][:, :, 0]
                    dve.tensor_tensor(second_halves(q, m), second_halves(q, m),
                                      blocks.unsqueeze(2).to_broadcast([P, CH * nb, m]), ALU.mult)\
                       .then_inc(q_step, 1)
                    if level > MASKED:
                        for n in range(64 // m):
                            rows = slice(2 * m * n, 2 * m * n + m)
                            done = dve.tensor_copy(ab[x][rows, :, 2 * m * n + m:2 * m * (n + 1)],
                                                   aux[rows, x, 0:m * CH].rearrange("p (c t) -> p c t", c=CH))
                        done.then_inc(sc_done, 1)
                        continue
                    dst = ab[x][:, :, :].rearrange("p c (b two m) -> p c b two m", two=2, m=m)[:, :, :, 1, :]
                    dve.copy_predicated(dst, mask_of(level),
                                        aux[:, x, 0:256].rearrange("p (c b m) -> p c b m", c=CH, m=m))\
                       .then_inc(sc_done, 1)
            elif s == LEVELS + 3:
                for x in range(2):
                    if x == 0:
                        dve.wait_ge(k_step, k_after(pair, LEVELS, 1, True))
                    dve.wait_ge(kv_full, 2 * pair + x + 1)
                    dve.tensor_copy(st[x][:, 0, :], aux[:, x, 0:P]).then_inc(st_ready, 1)
                    for c in range(CH - 1):
                        dve.wait_ge(st_ready, 8 * pair + 4 * x + c + 1)
                        dve.scalar_tensor_tensor(out=st[x][:, c + 1, :], in0=st[x][:, c, :],
                                                 scalar=tb[x][128][:, c:c + 1],
                                                 in1=aux[:, x, P * (c + 1):P * (c + 2)],
                                                 op0=ALU.mult, op1=ALU.add).then_inc(st_ready, 1)
            elif s == LEVELS + 4:
                dve.wait_ge(o2_ready, 2 * pair + 2)
                dve.tensor_scalar(om[:, 8:16], om[:, 0:8], 1.0 / P, EPS, ALU.mult, ALU.add)\
                   .then_inc(hm_ready, 1)
                dve.wait_ge(hm_ready, 2 * pair + 1)
                dve.reciprocal(om[:, 16:24], om[:, 8:16]).then_inc(hm_ready, 1)
            elif s == LEVELS + 5:
                for x in range(2):
                    dve.wait_ge(ot_turned, 2 * pair + x + 1)
                    dve.wait_ge(qg_ready, 2 + 4 * pair + 2 + x + 1)
                    dve.scalar_tensor_tensor(out=og[x][:, :], in0=aux[:, x, :],
                                             scalar=vec1[:, bass.ds(ONW + 2 * pair + x, 1)],
                                             in1=gb[par][x][:, :], op0=ALU.mult, op1=ALU.mult)\
                       .then_inc(zb_ready, 1)
                for x in range(2):
                    dve.wait_ge(zbhi_ready, 2 * pair + x + 1)
                    dve.tensor_tensor(zlob[:, 2 * par + x, :], og[x][:, :], zhib[:, 2 * par + x, :],
                                      ALU.subtract).then_inc(zblo_ready, 1)

        def b_scalar_step(act, s, pair, par):
            if s == 0:
                for x in range(2):
                    act.wait_ge(vt_full, 2 * pair + x + 1)
                    act.activation(vt[x][:, :, :], aux2[:, x, :].rearrange("p (c d) -> p c d", c=CH),
                                   ACT.Copy).then_inc(vt_ready, 1)
                    act.activation(vtm[x][:, :], aux[0:META, x, 0:P], ACT.Copy).then_inc(vt_ready, 1)
            elif s == LEVELS + 2:
                for x in range(2):
                    act.wait_ge(kt_full, 2 * pair + x + 1)
                    act.activation(kt[x][:, :, :], aux2[:, x, 0:3 * P].rearrange("p (c d) -> p c d", c=3),
                                   ACT.Copy).then_inc(kt_ready, 1)
                    act.activation(ktm[x][:, :], aux2[0:META, x, 3 * P:4 * P], ACT.Copy).then_inc(kt_ready, 1)
            elif s == LEVELS + 4:
                for x in range(2):
                    act.wait_ge(o_full, 2 * pair + x + 1)
                    for c in range(CH):
                        done = act.activation(sq[x][:, P * c:P * c + P], aux2[:, x, P * c:P * c + P],
                                              ACT.Square, accum_out=om[:, CH * x + c:CH * x + c + 1])
                    done.then_inc(o2_ready, 1)
                act.wait_ge(hm_ready, 2 * pair + 2)
                act.activation(om[:, 24:32], om[:, 16:24], ACT.Sqrt).then_inc(hr_ready, 1)
                act.wait_ge(hr_ready, pair + 1)
                for x in range(2):
                    for c in range(CH):
                        r = CH * x + c
                        done = act.activation(xn[x][:, P * c:P * c + P], aux2[:, x, P * c:P * c + P], ACT.Copy,
                                              scale=om[:, 24 + r:25 + r])
                    done.then_inc(on_ready, 1)
            elif s == LEVELS + 5:
                for x in range(2):
                    act.wait_ge(zb_ready, 1 + 2 * pair + x + 1)
                    act.activation(zhib[:, 2 * par + x, :], og[x][:, :], ACT.Copy).then_inc(zbhi_ready, 1)

        def pair_units(i, part):
            if part == "first":
                return 0, UB, PB
            k = 0 if part == "odd" else 1
            return 2 * i + 1 + k, UB + 8 + 8 * k + B_STEPS * i, PB + 8 + 8 * k + B_PIECES * i

        def pair_half(part, i):
            if part == "first":
                return UB // 2
            return UB // 2 + (4 if part == "odd" else 8) + (B_STEPS // 2) * i

        def c_base(i):
            return UC + C_STEPS * i

        ATT = [(p, b) for p in range(4) for b in range(CH)]
        STEP_OF = {}
        FREED = {}
        n_steps = 0
        for entry in C_PLAN:
            stage, index, kind, m, half, u = entry
            if kind == "vg":
                for q in range(4):
                    FREED[m + q] = n_steps + q + 1
                n_steps += 4
            else:
                n_steps += 1
                FREED[m] = n_steps
            STEP_OF[stage, index] = n_steps
        C_KIND = {}
        for stage, index, kind, m, half, u in C_PLAN:
            for q in range(4 if kind == "vg" else 1):
                C_KIND[m + q] = kind

        def c_done(i, u):
            return UC // 2 + (C_UNITS // 2) * i + u // 2 + 1

        def c_slots():
            att = 0
            order = []
            for entry in C_PLAN:
                stage, index, kind, m, half, u = entry
                for q in range(4 if kind == "vg" else 1):
                    side = []
                    if stage == "za" and index == 0:
                        side.append(("vtc", 0))
                        side.append(("ws", 0))
                    elif att < len(ATT) and stage in ("za", "u", "vg", "zg", "ga", "gg"):
                        side.append(("att", att))
                        att += 1
                    elif att < len(ATT) + 2 and att >= len(ATT):
                        side.append(("att", att))
                        att += 1
                    if stage in ("gg",) and index < 4:
                        side.append(("mix", index))
                    order.append((entry, q, side))
            return order

        C_ORDER = c_slots()

        X_DVE = 5

        def input_lo(eng, i, k, ready):
            eng.wait_ge(xhi_ready, 16 + 8 * i + k + 1)
            eng.tensor_tensor(xlo[:, k, META:T], h[:, k, META:T], xhi[:, k, META:T], ALU.subtract)\
               .then_inc(ready, 1)

        def input_wait(pe, i, k):
            if k < X_DVE:
                pe.wait_ge(xlo_ready, 16 + X_DVE * i + k + 1)
            else:
                pe.wait_ge(xlo_pool, (KT - X_DVE) * i + k - X_DVE + 1)

        GA_PIECES = next(e[3] for e in C_PLAN if e[0] == "ga") + AHEAD - 1

        block = ctx.enter_context(nc.Block())

        def load_chunk(sp, n, slot, src, kind, value):
            wait_apart(sp, "sp", (lo_ready, value))
            w = 256 if kind == "k8" else 512
            sp.dma_start(raw[slot][:, :].rearrange("p (k n) -> p k n", n=w), src)\
              .then_inc(raw_landed[slot], 16)

        w_in_a = a["pool_w_in"][0].rearrange("(k p) n -> p k n", p=P)
        w_grp = a["pool_w_grp"][0].rearrange("g (k p) n -> p (g k) n", p=P)
        w_out_a = a["pool_w_out"][0].rearrange("(k p) n -> p k n", p=P)
        w_in_b = a["hgrn_w_in"][0].rearrange("(k p) n -> p k n", p=P)
        w_out_b = a["hgrn_w_out"][0].rearrange("(k p) n -> p k n", p=P)
        w_in_c = a["w_in_2"].rearrange("l (k p) n -> p (l k) n", p=P)
        w_bra = a["w_branch_attn_2"].rearrange("l (k p) n -> p (l k) n", p=P)
        w_brg = a["w_branch_gmlp_2"].rearrange("l (k p) n -> p (l k) n", p=P)
        w_out_c = a["w_out_2"].rearrange("l (k p) n -> p (l k) n", p=P)

        @block.sync
        def _(sp):
            def const(dst, src):
                sp.dma_start(dst, src).then_inc(const_landed, 16)

            const(ident[:, :], a["c_ident"])
            const(rows1[NW0:FNW, :], a["norm_w"].rearrange("l (k p) -> (l k) p", p=P))
            const(rows1[FNW:PSC, :], a["final_norm_w"].rearrange("(k p) -> k p", p=P))
            const(rows1[PSC:ONW, :], a["pool_scale"].rearrange("l (k p) -> (l k) p", p=P))
            const(rows1[ONW:LBA, :], a["hgrn_o_norm"].rearrange("l (k p) -> (l k) p", p=P))
            const(rows1[LBA:N_V1, :], a["hgrn_lb_logits"].rearrange("l (k p) -> (l k) p", p=P))
            const(rows2[BIN:BOUT, :], a["b_in_2"].rearrange("l (k p) -> (l k) p", p=P))
            const(rows2[BOUT:LNG, :], a["b_out_2"].rearrange("l (k p) -> (l k) p", p=P))
            const(rows2[LNG:LNB, :], a["ln_g_2"].rearrange("l (k p) -> (l k) p", p=P))
            const(rows2[LNB:N_V2, :], a["ln_b_2"].rearrange("l (k p) -> (l k) p", p=P))
            const(pool_c[:, :, :], a["c_pool"])

            with sp.Fori(0, A_ITERS) as i:
                n = 0
                for gg in range(2):
                    g = 2 * i + gg
                    srcs = [("k8", w_in_a[:, :, bass.ds(512 * g + 256 * c, 256)]) for c in range(2)]
                    srcs += [("k8", w_in_a[:, :, bass.ds(E + 512 * g + 256 * c, 256)]) for c in range(2)]
                    srcs += [("k4", w_grp[:, bass.ds(GT * g, GT), :])]
                    srcs += [("k4", w_out_a[:, bass.ds(GT * g, GT), 512 * c:512 * c + 512]) for c in range(2)]
                    for kind, src in srcs:
                        load_chunk(sp, n, n % 2, src, kind, PA + A_PIECES * i + 2 * n - 2 + CREDIT)
                        n += 1

            def load_pair(i, part):
                pair, _, before = pair_units(i, part)
                for n, col in enumerate((E, 0, 2 * E, 3 * E)):
                    load_chunk(sp, n, n % 2, w_in_b[:, :, bass.ds(col + 256 * pair, 256)], "k8",
                               before + 2 * n - 2 + CREDIT)

            def load_out_b(g, before):
                for n in range(2):
                    load_chunk(sp, n, n % 2, w_out_b[:, bass.ds(GT * g, GT), 512 * n:512 * n + 512], "k4",
                               before + 2 * n - 2 + CREDIT)

            load_pair(None, "first")
            sp.wait_ge(xlo_ready, 16)
            sp.dma_start(masks[:, :], a["c_masks"]).then_inc(mask_landed, 16)
            with sp.Fori(0, NG - 1) as i:
                load_pair(i, "odd")
                load_pair(i, "even")
                load_out_b(i, PB + 24 + B_PIECES * i)
            load_pair(NG - 1, "odd")
            load_out_b(NG - 1, PB + 16 + B_PIECES * (NG - 1))

            with sp.Fori(0, DEPTH) as i:
                before = PC + C_PIECES * i
                chunks = []
                for stage, index, kind, m, half, u in C_PLAN:
                    if half or m % 2:
                        continue
                    if kind == "vg":
                        for c in range(2):
                            chunks.append((kind, w_in_c[:, bass.ds(8 * i + 4 * c, 4),
                                                        P * COL2["vg"]:P * COL2["vg"] + 512]))
                    elif stage == "wo":
                        chunks.append((kind, w_out_c[:, bass.ds(8 * i, 8), P * index:P * index + 256]))
                    elif kind == "k4":
                        src = w_bra if stage == "bra" else w_brg
                        chunks.append((kind, src[:, bass.ds(4 * i, 4), P * index:P * index + 512]))
                    else:
                        col = P * (COL2[stage] + index)
                        chunks.append((kind, w_in_c[:, bass.ds(8 * i, 8), col:col + 256]))
                for n, (kind, src) in enumerate(chunks):
                    value = before + CREDIT if n < 2 else before + 2 * n - 2 + CREDIT
                    load_chunk(sp, n, n % 2, src, kind, value)

            for c in range(CH):
                sp.wait_ge(ot_ready, 2 * c + 2)
                sp.dma_start(out[0][P * c:P * c + P, :], outt[:, c % 2, :]).then_inc(out_sent[c % 2], 16)
            for s in range(2):
                sp.wait_ge(out_sent[s], 16 * (CH // 2))

        @block.gpsimd
        def _(pool):
            pool.memset(ones_d[:, :], 1.0 / D).then_inc(ones_ready, 1)
            for buf in vpad + spad:
                pool.memset(buf[:, 0:META], 0.0).then_inc(pads_ready, 1)
            pool.wait_ge(xlo_ready, 16)
            for x in range(2):
                pool.memset(ab[x][:, :, :], 0.0).then_inc(a_zero, 1)
            with pool.Fori(0, NG) as i:
                for par in range(2):
                    pair = 2 * i + par
                    for level in range(1, LEVELS + 1):
                        for x in range(2):
                            pool.wait_ge(sc_full, 16 * pair + 2 * level + x + 1)
                            if level > 1:
                                pool.wait_ge(k_step, k_after(pair, level - 1, x, True))
                            m = 2 ** (level - 1)
                            both = at_level(x, par, m)[0]
                            n = both.shape[1]
                            k = kb[par][x][:, 0 if m < META else META:T]
                            pool.tensor_tensor(first_halves(k, m), first_halves(k, m),
                                               both[:, :, 1].unsqueeze(2).to_broadcast([P, n, m]), ALU.mult)\
                                .then_inc(k_step, 1)
                            pool.tensor_tensor(tb[x][2 * m][:, 0:n], both[:, :, 0], both[:, :, 1], ALU.mult)\
                                .then_inc(k_step, 1)
            pool.wait_ge(xn_ready, 8)
            pool.dma_start(nd[:, :], a["c_nd"]).then_inc(c_landed, 16)
            pool.dma_start(causal[:, :], a["c_causal"]).then_inc(c_landed, 16)
            with pool.Fori(0, DEPTH) as i:
                for k in range(X_DVE, KT):
                    input_lo(pool, i, k, xlo_pool)
                pool.wait_ge(lo_ready, PC + C_PIECES * i + 1 + CREDIT)
                for m in range(1, C_PIECES):
                    if m == AHEAD:
                        wait_apart(pool, "pool", (lin_done, c_base(i)),
                                   (lo_ready, PC + C_PIECES * i + AHEAD + CREDIT))
                        for kv in range(2):
                            for x in range(2):
                                pool.memset(kc[kv][HD * x:HD * x + HD, 1 - x, :], 0.0).then_inc(kz_ready, 1)
                        pool.wait_ge(kz_ready, 4 * i + 4)
                    split_lo(pool, C_KIND[m], m, PC + C_PIECES * i)
                    if GA_PIECES <= m < GA_PIECES + CH:
                        c = m - GA_PIECES
                        v = vn[:, c, :]
                        pool.wait_ge(vgn, 14 * i + 11 + c)
                        pool.tensor_tensor(v, v, gvg[:, :], ALU.mult).then_inc(vn_step, 1)
                        pool.wait_ge(vn_step, 8 * i + 2 * c + 1)
                        pool.tensor_tensor(v, v, bevg[:, :], ALU.add).then_inc(vn_step, 1)

        @block.tensor
        def _(pe):
            pe.wait_ge(const_landed, 16 * 11)
            pe.transpose(aux2[:, 0, 0:N_V1], rows1[:, :], ident[0:N_V1, 0:N_V1]).then_inc(vec_full, 1)
            pe.transpose(aux2[:, 1, 0:N_V2], rows2[:, :], ident[0:N_V2, 0:N_V2]).then_inc(vec_full, 1)
            pe.wait_ge(x_landed, 16 * (CH + 1))
            for k in range(KT):
                pe.wait_ge(acc_done[k % 2], k // 2)
                for c in range(CH):
                    pe.transpose(acc[k % 2][:, 0, P * c:P * c + P], xt[:, c, P * k:P * k + P], ident[:, :])
                pe.transpose(acc[k % 2][:, 1, 0:META], mt[:, P * k:P * k + P], ident[0:META, 0:META])\
                  .then_inc(lin_done, 1)
                if k == 1:
                    pe.wait_ge(ones_ready, 1)
                if k >= 2:
                    norm_tensor(pe, 0, T, [k - 2])
            norm_tensor(pe, 0, T, [KT - 2, KT - 1])

            with pe.Fori(0, A_ITERS) as i:
                for u, (gg, stage, n, kind, m, half) in enumerate(A_PLAN):
                    G = 2 * i + gg
                    pe.wait_ge(acc_done[u % 2], UA // 2 + (A_UNITS // 2) * i + u // 2)
                    pe.wait_ge(lo_ready, PA + A_PIECES * i + m + 1 + CREDIT)
                    if stage == "grp":
                        rhs = lambda k, t0, w: (uhi[:, k, t0:t0 + w], ulo[:, k, t0:t0 + w])
                        k_wait = (lambda k: pe.wait_ge(ulo_ready, 4 * G + k + 1)) if n == 0 else None
                    elif stage == "out":
                        rhs = lambda k, t0, w: (zhia[:, k, t0:t0 + w], zloa[:, k, t0:t0 + w])
                        k_wait = (lambda k: pe.wait_ge(zalo_ready, 4 * G + k + 1)) if n == 0 else None
                    else:
                        rhs, k_wait = of_x, (x_wait(pe, 0) if u == 0 else None)
                    unit(pe, u % 2, kind, m, half, KT if kind == "k8" else GT, rhs, T, k_wait)

            def b_pair(i, part, process):
                pair, u0, p0 = pair_units(i, part)
                slot = 0

                def side():
                    nonlocal slot
                    if process is not None and slot in STEP_AT:
                        b_tensor_step(pe, STEP_AT[slot], *process)
                    slot += 1

                for j, (what, x) in enumerate(PAIR_UNITS):
                    pe.wait_ge(acc_done[x], pair_half(part, i) + j // 2)
                    pe.wait_ge(lo_ready, p0 + j + 1 + CREDIT)
                    unit(pe, x, "k8", j, 0, KT, of_x, T if what in "fi" else SEQ,
                         x_wait(pe, 1) if part == "first" and j == 0 else None, side)
                    side()
                    if part == "first" and j == 0:
                        norm_tensor(pe, 1, T)

            def b_out(g, u0h, p0):
                z = lambda k, t0, w: (zhib[:, k, :], zlob[:, k, :])
                for n in range(OUT_UNITS):
                    pe.wait_ge(acc_done[n % 2], u0h + n // 2)
                    pe.wait_ge(lo_ready, p0 + n // 2 + 1 + CREDIT)
                    unit(pe, n % 2, "k4", n // 2, n % 2, GT, z, SEQ,
                         (lambda k: pe.wait_ge(zblo_ready, 4 * g + k + 1)) if n == 0 else None)

            b_pair(None, "first", None)
            pe.wait_ge(a_zero, 2)
            with pe.Fori(0, NG - 1) as i:
                b_pair(i, "odd", (2 * i, 0))
                b_pair(i, "even", (2 * i + 1, 1))
                b_out(i, UB // 2 + 12 + (B_STEPS // 2) * i, PB + 24 + B_PIECES * i)
            b_pair(NG - 1, "odd", (2 * (NG - 1), 0))
            for s in range(STEPS):
                b_tensor_step(pe, s, 2 * NG - 1, 1)
            b_out(NG - 1, UB // 2 + 8 + (B_STEPS // 2) * (NG - 1), PB + 16 + B_PIECES * (NG - 1))
            norm_tensor(pe, 2, SEQ)

            def att_tensor(i, s):
                base = 16 * i
                if s < len(ATT):
                    p, b = ATT[s]
                    if s == 0:
                        pe.wait_ge(kd_landed, 64 * i + 64)
                        pe.wait_ge(kz_ready, 4 * i + 4)
                        pe.wait_ge(ws_ready, i + 1)
                    pe.wait_ge(asc_ready, 1 + 2 * (base + s))
                    lo = 0 if b else P
                    pe.matmul(aux[:, 0, :].rearrange("p (x k) -> p x k", x=2)[:, :, lo:],
                              qc[:, p, P * b:P * b + P], kc[p // 2][:, :, P * (b - 1) + lo:P * (b + 1)],
                              start=True, stop=True).then_inc(asc_full, 1)
                if 1 <= s <= len(ATT):
                    b = ATT[s - 1][1]
                    pe.wait_ge(aprob, 4 * (base + s - 1) + 4)
                    pe.wait_ge(apt_ready, 1 + base + s - 1)
                    for x in range(2):
                        for kb_ in range(0 if b else 1, 2):
                            mm = pe.transpose(aux2[:, 0, P * (2 * x + kb_):P * (2 * x + kb_ + 1)],
                                              pr[(s - 1) % 2][:, x, P * kb_:P * kb_ + P], ident[:, :])
                    mm.then_inc(apt_full, 1)
                if 2 <= s:
                    p, b = ATT[s - 2]
                    pe.wait_ge(apt_ready, 1 + base + s - 1)
                    if b == 0:
                        pe.wait_ge(ya_ready, 1 + 4 * i + p)
                    for x in range(2):
                        kv = (2 * p + x) // 4
                        for kb_ in range(0 if b else 1, 2):
                            mm = pe.matmul(aux2[HD * x:HD * x + HD, 1, P * b:P * b + P],
                                           vtc[:, b - 1 + kb_, HD * kv:HD * kv + HD],
                                           pt[(s - 2) % 2][:, 2 * x + kb_, :],
                                           start=(kb_ == (0 if b else 1)), stop=(kb_ == 1))
                    mm.then_inc(ao_full, 1)

            def side_tensor(i, what, n):
                if what == "vtc":
                    pe.wait_ge(acc_done[1], c_done(i, 5))
                    for c in range(CH):
                        mm = pe.transpose(aux2[:, 0, P * c:P * c + P], vf[:, P * c:P * c + P], ident[:, :])
                    mm.then_inc(vtc_full, 1)
                elif what == "ws":
                    pe.wait_ge(lc_landed, 96 * i + 96)
                    for g in range(4):
                        mm = pe.transpose(aux2[:, 1, P * g:P * g + P], ws[:, g, :], ident[:, :])
                    mm.then_inc(ws_full, 1)
                elif what == "att":
                    if n == 0:
                        pe.wait_ge(vtc_ready, i + 1)
                    att_tensor(i, n)
                else:
                    pe.wait_ge(vn_step, 8 * i + 8)
                    pe.wait_ge(yg_step, 1 + 12 * i + max(3 * n - 2, 0))
                    for c in range(CH):
                        mm = pe.matmul(aux[:, 1, P * c:P * c + P], vn[:, c, P * n:P * n + P], wst[:, n, :],
                                       start=True, stop=True)
                    mm.then_inc(mix_full, 1)

            def mean_part(i, k):
                pe.wait_ge(wo_ready, 8 * i + k + 1)
                pe.matmul(aux[:, 1, :], ones_d[:, :], h[:, k, META:T], start=(k == 0),
                          stop=(k == KT - 1)).then_inc(mean_used, 1)

            with pe.Fori(0, DEPTH) as i:
                for (stage, index, kind, m, half, u), q, side in C_ORDER:
                    if q == 0:
                        pe.wait_ge(acc_done[u % 2], c_done(i, u) - 1)
                    pe.wait_ge(lo_ready, PC + C_PIECES * i + m + q + 1 + CREDIT)
                    if stage == "vg":
                        if q == 0:
                            pe.wait_ge(acc_done[1], c_done(i, u + 1) - 1)
                        hi, lo = piece(whi, kind, m + q), piece(wlo, kind, m + q)
                        for c in range(CH):
                            for kk in range(2):
                                k, t0 = 2 * q + kk, META + P * c
                                mm = products(pe, acc[c // 2][:, c % 2, :],
                                              (xhi[:, k, t0:t0 + P], xlo[:, k, t0:t0 + P]),
                                              (hi[:, kk, :], lo[:, kk, :]), k == 0, k == KT - 1)
                        mm.then_inc(lin_done, 1)
                    else:
                        k_wait = None
                        if stage in ("bra", "brg"):
                            y, ready = ((yah, yal), yalo_ready) if stage == "bra" else ((ygh, ygl), yglo_ready)
                            rhs = lambda k, t0, w: (y[0][:, k, :], y[1][:, k, :])
                            if index == 0:
                                k_wait = lambda k: pe.wait_ge(ready, 4 * i + k + 1)
                        elif stage == "wo":
                            rhs = lambda k, t0, w: (mhi[:, k, :], mlo[:, k, :])
                            if index == 0:
                                k_wait = lambda k: pe.wait_ge(mlo_ready, 8 * i + k + 1)
                        else:
                            rhs = of_x
                            if u == 0:
                                k_wait = lambda k: input_wait(pe, i, k)
                        unit(pe, u % 2, kind, m, half, GT if kind == "k4" else KT, rhs, SEQ, k_wait)
                        if stage == "wo" and index:
                            mean_part(i, index - 1)
                    for what, n in side:
                        side_tensor(i, what, n)
                mean_part(i, KT - 1)
                for k in range(KT):
                    pe.wait_ge(sq_ready, 24 + 8 * i + k + 1)
                    pe.matmul(aux[:, 0, :], ones_d[:, :], sq[k % 2][:, 0:SEQ], start=(k == 0),
                              stop=(k == KT - 1)).then_inc(sq_used, 1)

            pe.wait_ge(xn_ready, 8 + 8 * DEPTH)
            for c in range(CH):
                pe.wait_ge(ot_ready, max(0, 2 * (c - 1)))
                for k in range(KT):
                    mm = pe.transpose(acc[c % 2][:, k // 4, P * (k % 4):P * (k % 4) + P],
                                      h[:, k, META + P * c:META + P * c + P], ident[:, :])
                mm.then_inc(ot_full, 1)

        @block.scalar
        def _(act):
            act.sem_inc(apt_ready, 1)
            act.sem_inc(on_ready, 1)
            for c in range(CH):
                act.dma_start(xt[:, c, :], a["x"][0][P * c:P * c + P, :]).then_inc(x_landed, 16)
            act.dma_start(mt[:, :], a["meta_tokens"]).then_inc(x_landed, 16)
            act.wait_ge(lb_step, 3)
            act.activation(lbt[:, 3:5, :], lbt[:, 1:3, :], ACT.Exp).then_inc(lb_exp, 1)
            for k in range(KT):
                act.wait_ge(acc_done[k % 2], k // 2 + 1)
                weighted_hi(act, 0, k, NW0)
                square(act, 0, k, 0)
            for m in range(AHEAD):
                split_hi(act, "k8", m, 16 * (m // 4 + 1), None)
            root(act, 0, T)

            def a_split(i, m):
                m += AHEAD
                kinds = (["k8"] * 8 + ["k4"] * 6) * 2 + ["k8"] * AHEAD
                freed = [max(n + 1 for n, e in enumerate(A_PLAN) if e[4] == f) for f in range(A_PIECES)]
                at = freed[m - PIECES] if m >= PIECES else m - PIECES + 1
                split_hi(act, kinds[m], m, 4 * PA + 4 * A_PIECES * i + 16 * (m // 4 + 1),
                         UA + A_UNITS * i + at)

            def u_hi(G, n):
                act.wait_ge(win_step, 1 + 24 * G + 6 * n + 6)
                act.activation(uhi[:, n, :], pu[n % 2][:, :], ACT.Copy).then_inc(uhi_ready, 1)

            with act.Fori(0, A_ITERS) as i:
                for u, (gg, stage, n, kind, m, half) in enumerate(A_PLAN):
                    G, slot = 2 * i + gg, u % 2
                    if stage != "out":
                        act.wait_ge(lin_done, UA + A_UNITS * i + u + 1)
                    if stage == "gate":
                        act.wait_ge(acc_done[slot], UA // 2 + (A_UNITS // 2) * i + u // 2 + 1)
                        if n >= 2:
                            act.wait_ge(ga_ready, 4 * G + n - 1)
                        act.activation(sga[slot][:, :], ga[:, n, :], ACT.Sigmoid).then_inc(siga_ready, 1)
                    if stage == "v" and n or stage == "gate" and n == 0:
                        u_hi(G, (n - 1) % 4)
                    if stage == "grp":
                        act.wait_ge(acc_done[slot], UA // 2 + (A_UNITS // 2) * i + u // 2 + 1)
                        act.activation(zhia[:, n, :], pz[slot][:, :], ACT.Copy).then_inc(zahi_ready, 1)
                    if kind == "k8" or half == 1:
                        a_split(i, m)
            for k in range(KT):
                act.wait_ge(acc_done[k % 2], UB // 2 - 4 + k // 2 + 1)
                weighted_hi(act, 1, k, NW1)
            for k in range(KT):
                square(act, 1, k, 0)
            root(act, 1, T)

            def b_split(p0, m, kind, freed):
                split_hi(act, kind, m % 4, 4 * p0 + 16 * (m // 4 + 1), freed)

            def b_pair(i, part, process, after):
                pair, u0, p0 = pair_units(i, part)
                par = int(part == "odd")
                slot = 0

                def side():
                    nonlocal slot
                    if process is not None and slot in STEP_AT:
                        b_scalar_step(act, STEP_AT[slot], *process)
                    slot += 1

                for j, (what, x) in enumerate(PAIR_UNITS):
                    side()
                    side()
                    if what != "i":
                        act.wait_ge(acc_done[x], pair_half(part, i) + j // 2 + 1)
                    if what == "f":
                        act.wait_ge(qg_ready, 4 * pair + x + 1)
                        act.wait_ge(k_ready, 1 + 2 * pair)
                        act.activation(sgb[x][:, :], snb[x][:, :], ACT.Sigmoid).then_inc(sgb_ready, 1)
                        act.activation(snb[x][:, :], snb[x][:, :], ACT.Sigmoid, scale=-1.0)\
                           .then_inc(snb_ready, 1)
                    elif what == "q":
                        act.wait_ge(f_ready, 2 * pair + x + 1)
                        act.activation(sgb[x][:, 0:SEQ], qb[par][x][:, :], ACT.Sigmoid).then_inc(sgb_ready, 1)
                    elif what == "g":
                        act.wait_ge(qg_ready, 2 + 4 * pair + x + 1)
                        act.activation(sgb[x][:, 0:SEQ], gb[par][x][:, :], ACT.Sigmoid).then_inc(sgb_ready, 1)
                    m = j + AHEAD
                    b_split(p0, m, "k8" if m < 8 else after, u0 + m - 3)

            def b_out_splits(u0, p0, ahead):
                for n in range(1, OUT_UNITS, 2):
                    m = n // 2 + AHEAD
                    if m < 4 or ahead:
                        act.wait_ge(lin_done, u0 + n + 1)
                        freed = u0 if m == 3 else u0 + 2 * (m - 3)
                        b_split(p0, m, "k4" if m < 4 else "k8", freed)

            b_pair(None, "first", None, "k8")
            with act.Fori(0, NG - 1) as i:
                b_pair(i, "odd", (2 * i, 0), "k8")
                b_pair(i, "even", (2 * i + 1, 1), "k4")
                b_out_splits(UB + 24 + B_STEPS * i, PB + 24 + B_PIECES * i, True)
            b_pair(NG - 1, "odd", (2 * (NG - 1), 0), "k4")
            for s in range(STEPS):
                b_scalar_step(act, s, 2 * NG - 1, 1)
            b_out_splits(UB + 16 + B_STEPS * (NG - 1), PB + 16 + B_PIECES * (NG - 1), False)
            norm_scalar(act, 2, SEQ, lambda e, k: e.wait_ge(acc_done[k % 2], UC // 2 - 4 + k // 2 + 1))

            def att_scalar(i, s):
                base = 16 * i
                if s < len(ATT):
                    p, b = ATT[s]
                    lo, z = (0 if b else P), s % 2
                    act.wait_ge(arow, 4 * (base + s) + 4)
                    for x in range(2):
                        act.activation(pr[z][:, x, lo:], sc[z][:, x, lo:], ACT.Exp,
                                       bias=sm[z][:, 2, x:x + 1], accum_out=sm[z][:, 4, x:x + 1])\
                           .then_inc(aexp, 1)
                    act.activation(sm[z][:, 5, :], sm[z][:, 3, :], ACT.Exp).then_inc(aexp, 1)

            def att_scalar_turned(i, s):
                if 1 <= s <= len(ATT):
                    b = ATT[s - 1][1]
                    act.wait_ge(apt_full, 16 * i + s)
                    z, first = (s - 1) % 2, (0 if b else 1)
                    act.activation(pt[z][:, :, :].rearrange("p (x k) q -> p x k q", x=2)[:, :, first:, :],
                                   aux2[:, 0, :].rearrange("p (x k q) -> p x k q", x=2, k=2)[:, :, first:, :],
                                   ACT.Copy).then_inc(apt_ready, 1)
                if s >= 2 and ATT[s - 2][1] == CH - 1:
                    p = ATT[s - 2][0]
                    act.wait_ge(ya_ready, 1 + 4 * i + p + 1)
                    act.activation(yah[:, p, :], sq[p % 2][:, 0:SEQ], ACT.Copy).then_inc(yahi_ready, 1)

            with act.Fori(0, DEPTH) as i:
                def bias(col):
                    return vec2[:, bass.ds(NIN2 * i + col, 1)]

                act.wait_ge(lin_done, c_base(i))
                for k in range(KT):
                    act.wait_ge(xn_ready, 8 * i + k + 1)
                    act.activation(xhi[:, k, META:T], h[:, k, META:T], ACT.Copy).then_inc(xhi_ready, 1)

                def rows(dst, src):
                    act.dma_start(dst, src).then_inc(lc_landed, 16)

                def row(name, w):
                    return a[name][bass.ds(i, 1), :].to_broadcast([P, w])

                rows(ws, a["w_spatial_2"].rearrange("l g t s -> t (l g) s")[:, bass.ds(4 * i, 4), :])
                rows(bvg[:, :], a["b_in_2"][bass.ds(i, 1), P * COL2["vg"]:P * COL2["vg"] + 512]
                     .to_broadcast([P, 512]))
                rows(gvg[:, :], row("gmlp_ln_g_2", 512))
                rows(bevg[:, :], row("gmlp_ln_b_2", 512))
                rows(bsp[:, :, :].rearrange("p g t -> p (g t)"),
                     a["b_spatial_2"].rearrange("l g t -> l (g t)")[bass.ds(i, 1), :].to_broadcast([P, 512]))
                rows(sinks[:, :], row("attn_sinks_2", 8))
                for (stage, index, kind, m, half, u), q, side in C_ORDER:
                    slot, n = u % 2, index % 4
                    psum = acc[slot][:, 0, :]
                    b = bias(COL2[stage] + index) if stage in COL2 else None
                    step = STEP_OF[stage, index] - (3 - q if stage == "vg" else 0)
                    if stage not in ("bra", "brg"):
                        act.wait_ge(lin_done, c_base(i) + step)
                    if stage == "q":
                        act.activation(qc[:, n, :], psum, ACT.Identity, scale=ATT_SCALE,
                                       bias=qbias[:, bass.ds(4 * i + n, 1)]).then_inc(acc_done[slot], 1)
                    elif stage in ("k", "v"):
                        act.activation((kf if stage == "k" else vf)[:, :], psum, ACT.Identity, bias=b)\
                           .then_inc(acc_done[slot], 1)
                        if stage == "k":
                            act.wait_ge(acc_done[slot], c_done(i, u))
                            for kv in range(2):
                                for x in range(2):
                                    act.dma_start(kc[kv][HD * x:HD * x + HD, x, :],
                                                  kf[HD * kv:HD * kv + HD, :]).then_inc(kd_landed, 16)
                    elif stage in ("za", "zg"):
                        act.activation(sgc[slot][:, :], psum, ACT.Sigmoid, bias=b).then_inc(sigc_ready, 1)
                    elif stage == "u":
                        act.activation(ug[:, n, :], psum, ACT.Gelu, bias=b).then_inc(acc_done[slot], 1)
                    elif stage in ("ga", "gg"):
                        if index == 4:
                            act.wait_ge(mlo_ready, 8 * i + 4)
                        act.activation((gac if stage == "ga" else ggc)[:, n, :], psum, ACT.Sigmoid, bias=b)\
                           .then_inc(acc_done[slot], 1)
                    elif stage == "wo":
                        if index >= 2:
                            act.wait_ge(wo_ready, 8 * i + index - 1)
                        act.activation(xn[slot][:, 0:SEQ], psum, ACT.Identity,
                                       bias=vec2[:, bass.ds(BOUT + 8 * i + index, 1)])\
                           .then_inc(acc_done[slot], 1)
                    for what, s in side:
                        if what == "att":
                            att_scalar(i, s)
                    for what, s in side:
                        if what == "att":
                            att_scalar_turned(i, s)
                        elif what == "vtc":
                            act.wait_ge(vtc_full, i + 1)
                            act.activation(vtc[:, :, :], aux2[:, 0, :].rearrange("p (c d) -> p c d", c=CH),
                                           ACT.Copy).then_inc(vtc_ready, 1)
                        elif what == "mix":
                            act.wait_ge(yg_step, 1 + 12 * i + 3 * s + 3)
                            act.activation(ygh[:, s, :], xn[s % 2][:, 0:SEQ], ACT.Copy).then_inc(yghi_ready, 1)
                    if stage == "vg" and q == 3:
                        for c in range(CH):
                            if c % 2 == 0:
                                act.wait_ge(vgb_ready, 2 * i + c // 2 + 1)
                            else:
                                act.wait_ge(acc_done[c // 2], c_done(i, u + c // 2))
                            act.activation(vn[:, c, :], vn[:, c, :], ACT.Gelu).then_inc(vgg_ready, 1)
                    if stage == "zg" and n == 0:
                        act.wait_ge(vgn, 14 * i + 10)
                        act.activation(vgr[:, :], vgr[:, :], ACT.Sqrt).then_inc(vgr_ready, 1)
                    if stage == "brg":
                        act.wait_ge(m_ready, 8 * i + index + 1)
                        act.activation(mhi[:, index, :], gac[:, n, :], ACT.Copy).then_inc(mhi_ready, 1)
                for k in range(KT):
                    act.wait_ge(xc_ready, 8 * i + k + 1)
                    if k >= 2:
                        act.wait_ge(sq_used, 24 + 8 * i + k - 1)
                    act.activation(sq[k % 2][:, 0:SEQ], h[:, k, META:T], ACT.Square).then_inc(sq_ready, 1)
                act.wait_ge(ms_ready, 6 + 2 * i + 2)
                act.activation(rstd[:, 0:SEQ], rstd[:, 0:SEQ], ACT.Sqrt).then_inc(rstd_ready, 1)

            for c in range(CH):
                act.wait_ge(ot_full, c + 1)
                if c >= 2:
                    act.wait_ge(out_sent[c % 2], 16 * (c // 2))
                act.activation(outt[:, c % 2, 0:512], acc[c % 2][:, 0, :], ACT.Copy).then_inc(ot_ready, 1)
                act.activation(outt[:, c % 2, 512:1024], acc[c % 2][:, 1, :], ACT.Copy).then_inc(ot_ready, 1)

        @block.vector
        def _(dve):
            for counted in (zb_ready, asc_ready, ya_ready, yg_step, k_ready, win_step,
                            qg_ready, qg_ready):
                dve.sem_inc(counted, 1)
            dve.memset(lbt[:, 7, :], 0.0).then_inc(lo_ready, CREDIT)
            dve.wait_ge(vec_full, 1)
            dve.tensor_copy(vec1[:, :], aux2[:, 0, 0:N_V1]).then_inc(vec_ready, 1)
            dve.wait_ge(vec_full, 2)
            dve.tensor_copy(vec2[:, :], aux2[:, 1, 0:N_V2]).then_inc(vec_ready, 1)
            dve.wait_ge(vec_ready, 2)
            for l in range(DEPTH):
                dve.tensor_scalar(qbias[:, 4 * l:4 * l + 4], vec2[:, NIN2 * l:NIN2 * l + 4], ATT_SCALE, None,
                                  ALU.mult).then_inc(vec_ready, 1)
            l0, l1 = vec1[:, LBA:LBA + NH], vec1[:, LBB:LBB + NH]
            dve.tensor_tensor(lbt[:, 0, :], l0, l1, ALU.max).then_inc(lb_step, 1)
            dve.wait_ge(lb_step, 1)
            dve.tensor_tensor(lbt[:, 1, :], l0, lbt[:, 0, :], ALU.subtract).then_inc(lb_step, 1)
            dve.tensor_tensor(lbt[:, 2, :], l1, lbt[:, 0, :], ALU.subtract).then_inc(lb_step, 1)
            dve.wait_ge(lb_exp, 1)
            dve.tensor_tensor(lbt[:, 5, :], lbt[:, 3, :], lbt[:, 4, :], ALU.add).then_inc(lb_step, 1)
            dve.wait_ge(lb_step, 4)
            dve.reciprocal(lbt[:, 6, :], lbt[:, 5, :]).then_inc(lb_step, 1)
            dve.wait_ge(lb_step, 5)
            dve.tensor_tensor(lbt[:, 0, :], lbt[:, 3, :], lbt[:, 6, :], ALU.mult).then_inc(lb_step, 1)
            dve.tensor_tensor(lbt[:, 1, :], lbt[:, 4, :], lbt[:, 6, :], ALU.mult).then_inc(lb_step, 1)
            dve.wait_ge(lb_step, 7)
            dve.tensor_tensor(lbt[:, 2, :], lbt[:, 0, :], lbt[:, 1, :], ALU.add).then_inc(lb_step, 1)
            dve.wait_ge(lb_step, 8)
            dve.tensor_tensor(lb[:, :], lbt[:, 2, :], lbt[:, 0, :], ALU.subtract).then_inc(lb_step, 1)
            dve.wait_ge(lb_step, 9)
            dve.tensor_scalar(oml[:, :], lb[:, :], -1.0, 1.0, ALU.mult, ALU.add).then_inc(lb_step, 1)

            for k in range(KT):
                dve.wait_ge(lin_done, k + 1)
                dve.tensor_copy(h[:, k, META:T], acc[k % 2][:, 0, :])
                dve.tensor_copy(h[:, k, 0:META], acc[k % 2][:, 1, 0:META]).then_inc(acc_done[k % 2], 1)
                if k:
                    weighted_lo(dve, 0, k - 1, NW0)
            weighted_lo(dve, 0, KT - 1, NW0)
            for m in range(AHEAD):
                split_lo(dve, "k8", m, PA)
            weighted_inverse(dve, 0)

            def u_lo(G, n):
                dve.wait_ge(uhi_ready, 4 * G + n + 1)
                dve.tensor_tensor(ulo[:, n, :], pu[n % 2][:, :], uhi[:, n, :], ALU.subtract)\
                   .then_inc(ulo_ready, 1)

            def silu_a(G, n):
                dve.wait_ge(siga_ready, 4 * G + n + 1)
                dve.tensor_tensor(ga[:, n, :], ga[:, n, :], sga[n % 2][:, :], ALU.mult).then_inc(ga_ready, 1)

            A_KINDS = (["k8"] * 8 + ["k4"] * 6) * 2 + ["k8"] * AHEAD
            with dve.Fori(0, A_ITERS) as i:
                for u, (gg, stage, n, kind, m, half) in enumerate(A_PLAN):
                    G, slot = 2 * i + gg, u % 2
                    done = UA // 2 + (A_UNITS // 2) * i + u // 2 + 1
                    if stage != "out":
                        dve.wait_ge(lin_done, UA + A_UNITS * i + u + 1)
                    if stage == "v":
                        v, w0 = vpad[slot], 24 * G + 6 * n
                        if n == 0:
                            dve.wait_ge(pads_ready, 4)
                        dve.wait_ge(win_step, 1 + w0 - 6 * min(n, 1))
                        dve.tensor_tensor(halves(v[:, META:META + T]), acc_all(slot), halves(rstd[:, :]),
                                          ALU.mult).then_inc(acc_done[slot], 1)
                        dve.wait_ge(acc_done[slot], done)

                        def coef(j):
                            return pool_c[:, bass.ds(G, 1), j:j + 1].rearrange("p g c -> p (g c)")

                        def shifted(buf, by):
                            return buf[:, META - by:META - by + T]

                        if n:
                            dve.wait_ge(win_step, 1 + w0)
                        dve.tensor_tensor(shifted(spad[0], 0), shifted(v, 1), shifted(v, 0), ALU.add)\
                           .then_inc(win_step, 1)
                        for j, by in enumerate((2, 4, 8)):
                            dve.wait_ge(win_step, 1 + w0 + j + 1)
                            src, dst = spad[j % 2], spad[1 - j % 2]
                            dve.scalar_tensor_tensor(out=shifted(dst, 0), in0=shifted(src, by), scalar=coef(j),
                                                     in1=shifted(src, 0), op0=ALU.mult, op1=ALU.add)\
                               .then_inc(win_step, 1)
                        dve.wait_ge(win_step, 1 + w0 + 4)
                        dve.tensor_tensor(spad[1][:, META:2 * META], spad[1][:, META:2 * META],
                                          pool_c[:, bass.ds(G, 1), 4:20].rearrange("p g c -> p (g c)"),
                                          ALU.mult).then_inc(win_step, 1)
                        dve.wait_ge(win_step, 1 + w0 + 5)
                        if n >= 2:
                            dve.wait_ge(ulo_ready, 4 * G + n - 1)
                        dve.scalar_tensor_tensor(out=pu[slot][:, :], in0=shifted(spad[1], 0), scalar=coef(3),
                                                 in1=shifted(v, 0), op0=ALU.mult, op1=ALU.subtract)\
                           .then_inc(win_step, 1)
                    elif stage == "gate":
                        dve.tensor_tensor(halves(ga[:, n, :]), acc_all(slot), halves(rstd[:, :]),
                                          ALU.mult).then_inc(acc_done[slot], 1)
                        if n:
                            silu_a(G, n - 1)
                    elif stage == "grp":
                        if n == 0:
                            silu_a(G, GT - 1)
                        dve.wait_ge(ga_ready, 4 * G + n + 1)
                        if n >= 2:
                            dve.wait_ge(zalo_ready, 4 * G + n - 1)
                        dve.scalar_tensor_tensor(out=halves(pz[slot][:, :]), in0=acc_all(slot),
                                                 scalar=vec1[:, bass.ds(PSC + GT * G + n, 1)],
                                                 in1=halves(ga[:, n, :]), op0=ALU.mult, op1=ALU.mult)\
                           .then_inc(acc_done[slot], 1)
                    else:
                        dve.wait_ge(lin_done, UA + A_UNITS * i + u + 1)
                        dve.tensor_tensor(halves(h[:, n, :]), acc_all(slot), halves(h[:, n, :]), ALU.add)\
                           .then_inc(acc_done[slot], 1)
                    if stage == "v" and n or stage == "gate" and n == 0:
                        u_lo(G, (n - 1) % 4)
                    if stage == "grp":
                        dve.wait_ge(zahi_ready, 4 * G + n + 1)
                        dve.tensor_tensor(zloa[:, n, :], pz[slot][:, :], zhia[:, n, :], ALU.subtract)\
                           .then_inc(zalo_ready, 1)
                    if kind == "k8" or half == 1:
                        split_lo(dve, A_KINDS[m + AHEAD], m + AHEAD, PA + A_PIECES * i)
            for k in range(KT):
                weighted_lo(dve, 1, k, NW1)
            weighted_inverse(dve, 1)

            def b_pair(i, part, process, after):
                pair, u0, p0 = pair_units(i, part)
                par = int(part == "odd")
                slot = 0

                def side():
                    nonlocal slot
                    if process is not None and slot in STEP_AT:
                        b_vector_step(dve, STEP_AT[slot], *process)
                    slot += 1

                def finish(j):
                    what, x = PAIR_UNITS[j]
                    col = bass.ds(2 * pair + x, 1)
                    if what == "f":
                        dve.wait_ge(sgb_ready, 6 * pair + x + 1)
                        dve.tensor_scalar(fb[par][x][:, :], sgb[x][:, :], oml[:, col], lb[:, col],
                                          ALU.mult, ALU.add).then_inc(f_ready, 1)
                        dve.wait_ge(snb_ready, 2 * pair + x + 1)
                        dve.tensor_scalar(kb[par][x][:, :], snb[x][:, :], oml[:, col], None, ALU.mult)\
                           .then_inc(k_ready, 1)
                    elif what in "qg":
                        dve.wait_ge(sgb_ready, 6 * pair + (3 if what == "q" else 5) + x)
                        dst = (qb if what == "q" else gb)[par][x]
                        dve.tensor_tensor(dst[:, :], dst[:, :], sgb[x][:, 0:SEQ], ALU.mult)\
                           .then_inc(qg_ready, 1)

                for j, (what, x) in enumerate(PAIR_UNITS):
                    side()
                    dve.wait_ge(lin_done, u0 + j + 1)
                    if what in "fi":
                        dst = (snb if what == "f" else ib[par])[x]
                        if what == "f":
                            dve.wait_ge(k_ready, 1 + 2 * pair)
                        dve.tensor_tensor(halves(dst[:, :]), acc_all(x), halves(rstd[:, :]), ALU.mult)\
                           .then_inc(acc_done[x], 1)
                    else:
                        dst = (qb if what == "q" else gb)[par][x]
                        dve.tensor_tensor(dst[:, :], acc[x][:, 0, :], rstd[:, META:T], ALU.mult)\
                           .then_inc(acc_done[x], 1)
                    if j:
                        finish(j - 1)
                    side()
                    m = j + AHEAD
                    split_lo_at(p0, m, "k8" if m < 8 else after)
                finish(7)

            def split_lo_at(p0, m, kind):
                dve.wait_ge(hi_ready, p0 + m + 1)
                dve.tensor_tensor(piece(wlo, kind, m), raw_view(kind, m), piece(whi, kind, m),
                                  ALU.subtract).then_inc(lo_ready, 1)

            def b_out(u0, p0, ahead):
                for n in range(OUT_UNITS):
                    dve.wait_ge(lin_done, u0 + n + 1)
                    dve.tensor_tensor(h[:, n, META:T], acc[n % 2][:, 0, :], h[:, n, META:T], ALU.add)\
                       .then_inc(acc_done[n % 2], 1)
                    m = n // 2 + AHEAD
                    if n % 2 and (m < 4 or ahead):
                        split_lo_at(p0, m, "k4" if m < 4 else "k8")

            b_pair(None, "first", None, "k8")
            dve.wait_ge(mask_landed, 16)
            dve.wait_ge(a_zero, 2)
            with dve.Fori(0, NG - 1) as i:
                b_pair(i, "odd", (2 * i, 0), "k8")
                b_pair(i, "even", (2 * i + 1, 1), "k4")
                b_out(UB + 24 + B_STEPS * i, PB + 24 + B_PIECES * i, True)
            b_pair(NG - 1, "odd", (2 * (NG - 1), 0), "k4")
            for s in range(STEPS):
                b_vector_step(dve, s, 2 * NG - 1, 1)
            b_out(UB + 16 + B_STEPS * (NG - 1), PB + 16 + B_PIECES * (NG - 1), False)
            norm_vector(dve, 2, SEQ, FNW)

            def att_vector(i, s):
                base = 16 * i
                if s < len(ATT):
                    p, b = ATT[s]
                    lo, z = (0 if b else P), s % 2
                    dve.wait_ge(asc_full, base + s + 1)
                    for x in range(2):
                        dve.scalar_tensor_tensor(out=sc[z][:, x, lo:], in0=nd[:, lo:], scalar=SLOPES[2 * p + x],
                                                 in1=aux[:, 0, 2 * P * x + lo:2 * P * (x + 1)],
                                                 op0=ALU.mult, op1=ALU.add).then_inc(asc_ready, 1)
                    dve.wait_ge(asc_ready, 1 + 2 * (base + s) + 2)
                    dve.tensor_reduce(sm[z][:, 0, :], sc[z][:, :, lo:], AX_X, ALU.max).then_inc(arow, 1)
                    dve.wait_ge(arow, 4 * (base + s) + 1)
                    sink = sinks[:, 2 * p:2 * p + 2]
                    dve.tensor_tensor(sm[z][:, 1, :], sm[z][:, 0, :], sink, ALU.max).then_inc(arow, 1)
                    dve.wait_ge(arow, 4 * (base + s) + 2)
                    dve.tensor_scalar(sm[z][:, 2, :], sm[z][:, 1, :], -1.0, None, ALU.mult).then_inc(arow, 1)
                    dve.tensor_tensor(sm[z][:, 3, :], sink, sm[z][:, 1, :], ALU.subtract).then_inc(arow, 1)

            def att_vector_norm(i, s):
                base = 16 * i
                if s < len(ATT):
                    p, b = ATT[s]
                    lo, z = (0 if b else P), s % 2
                    dve.wait_ge(aexp, 3 * (base + s) + 3)
                    dve.tensor_tensor(sm[z][:, 6, :], sm[z][:, 4, :], sm[z][:, 5, :], ALU.add).then_inc(aprob, 1)
                    dve.wait_ge(aprob, 4 * (base + s) + 1)
                    dve.reciprocal(sm[z][:, 7, :], sm[z][:, 6, :]).then_inc(aprob, 1)
                    dve.wait_ge(aprob, 4 * (base + s) + 2)
                    for x in range(2):
                        dve.tensor_scalar(pr[z][:, x, lo:], pr[z][:, x, lo:], sm[z][:, 7, x:x + 1], None,
                                          ALU.mult).then_inc(aprob, 1)
                if s >= 2 and ATT[s - 2][1] == CH - 1:
                    p = ATT[s - 2][0]
                    dve.wait_ge(ao_full, base + s - 1)
                    dve.tensor_tensor(sq[p % 2][:, 0:SEQ], aux2[:, 1, :], za[:, p, :], ALU.mult)\
                       .then_inc(ya_ready, 1)
                    dve.wait_ge(yahi_ready, 4 * i + p + 1)
                    dve.tensor_tensor(yal[:, p, :], sq[p % 2][:, 0:SEQ], yah[:, p, :], ALU.subtract)\
                       .then_inc(yalo_ready, 1)

            def mix_vector(i, g):
                y, w0 = xn[g % 2][:, 0:SEQ], 12 * i + 3 * g
                dve.wait_ge(mix_full, 4 * i + g + 1)
                dve.tensor_tensor(y.rearrange("p (c t) -> p c t", c=CH),
                                  aux[:, 1, :].rearrange("p (c t) -> p c t", c=CH),
                                  bsp[:, g:g + 1, :].to_broadcast([P, CH, P]), ALU.add).then_inc(yg_step, 1)
                dve.wait_ge(yg_step, 1 + w0 + 1)
                dve.tensor_tensor(y, y, ug[:, g, :], ALU.mult).then_inc(yg_step, 1)
                dve.wait_ge(yg_step, 1 + w0 + 2)
                dve.tensor_tensor(y, y, zg[:, g, :], ALU.mult).then_inc(yg_step, 1)
                dve.wait_ge(yghi_ready, 4 * i + g + 1)
                dve.tensor_tensor(ygl[:, g, :], y, ygh[:, g, :], ALU.subtract).then_inc(yglo_ready, 1)

            def vg_norm(i):
                w0 = 14 * i
                for c in range(CH):
                    dve.wait_ge(vgg_ready, 4 * i + c + 1)
                    dve.bn_stats(vgst[:, c, 0:6], vn[:, c, :]).then_inc(vgn, 1)
                for c in range(CH):
                    wait_apart(dve, "dve", (vgn, w0 + 4 + c))
                    dve.bn_aggr(vgst[:, c, 6:8], vgst[:, c, 0:6]).then_inc(vgn, 1)
                dve.wait_ge(vgn, w0 + 8)
                dve.tensor_scalar(vgr[:, :], vgst[:, :, 7], LN_EPS, None, ALU.add).then_inc(vgn, 1)
                dve.wait_ge(vgn, w0 + 9)
                dve.reciprocal(vgr[:, :], vgr[:, :]).then_inc(vgn, 1)

            def vg_scale(i):
                dve.wait_ge(vgr_ready, i + 1)
                for c in range(CH):
                    v = vn[:, c, :]
                    dve.tensor_scalar(v, v, vgst[:, c, 6:7], vgr[:, c:c + 1], ALU.subtract, ALU.mult)\
                       .then_inc(vgn, 1)

            def c_split(i, m):
                landed = 4 * PC + 16 * (m // 4 + 1) + (16 * 14 if (m // 2) % 2 == 0 else 16 * 13) * i
                dve.wait_ge(raw_landed[(m // 2) % RAW], landed)
                dve.wait_ge(lin_done, c_base(i) + (FREED[m - PIECES] if m >= PIECES else 0))
                dve.tensor_copy(piece(whi, C_KIND[m], m), raw_view(C_KIND[m], m)).then_inc(hi_ready, 1)

            with dve.Fori(0, DEPTH) as i:
                c_split(i, 0)
                split_lo(dve, C_KIND[0], 0, PC + C_PIECES * i)
                for k in range(X_DVE):
                    input_lo(dve, i, k, xlo_ready)
                for m in range(1, AHEAD):
                    c_split(i, m)
                for (stage, index, kind, m, half, u), q, side in C_ORDER:
                    slot, n = u % 2, index % 4
                    psum = acc[slot][:, 0, :]
                    step = c_base(i) + STEP_OF[stage, index]
                    if stage in ("za", "zg"):
                        dve.wait_ge(sigc_ready, 8 * i + (4 if stage == "zg" else 0) + n + 1)
                        dve.scalar_tensor_tensor(out=(za if stage == "za" else zg)[:, n, :], in0=psum,
                                                 scalar=vec2[:, bass.ds(NIN2 * i + COL2[stage] + n, 1)],
                                                 in1=sgc[slot][:, :], op0=ALU.add, op1=ALU.mult)\
                           .then_inc(acc_done[slot], 1)
                    elif stage == "vg" and q == 3:
                        dve.wait_ge(lin_done, step)
                        dve.wait_ge(lc_landed, 96 * i + 96)
                        for c in range(CH):
                            dve.tensor_tensor(vn[:, c, :], acc[c // 2][:, c % 2, :], bvg[:, :], ALU.add)\
                               .then_inc(acc_done[c // 2] if c % 2 else vgb_ready, 1)
                    elif stage == "bra":
                        dve.wait_ge(lin_done, step)
                        dve.tensor_tensor(gac[:, n, :], psum, gac[:, n, :], ALU.mult).then_inc(acc_done[slot], 1)
                    elif stage == "brg":
                        dve.wait_ge(lin_done, step)
                        dve.tensor_tensor(ggc[:, n, :], psum, ggc[:, n, :], ALU.mult).then_inc(acc_done[slot], 1)
                        dve.wait_ge(acc_done[slot], c_done(i, u))
                        dve.tensor_tensor(gac[:, n, :], gac[:, n, :], ggc[:, n, :], ALU.add)\
                           .then_inc(m_ready, 1)
                    elif stage == "wo":
                        dve.wait_ge(acc_done[slot], c_done(i, u))
                        dve.scalar_tensor_tensor(out=h[:, index, META:T], in0=h[:, index, META:T],
                                                 scalar=ALPHA, in1=xn[slot][:, 0:SEQ], op0=ALU.mult,
                                                 op1=ALU.add).then_inc(wo_ready, 1)
                    for what, s in side:
                        if what == "att":
                            att_vector(i, s)
                    if (kind != "k4" or half == 1) and m + q + AHEAD < C_PIECES:
                        c_split(i, m + q + AHEAD)
                    for what, s in side:
                        if what == "att":
                            att_vector_norm(i, s)
                        elif what == "ws":
                            dve.wait_ge(c_landed, 32)
                            dve.wait_ge(ws_full, i + 1)
                            dve.tensor_tensor(wst[:, :, :], aux2[:, 1, :].rearrange("p (g t) -> p g t", g=4),
                                              causal[:, None, :].to_broadcast([P, 4, P]), ALU.mult)\
                               .then_inc(ws_ready, 1)
                        elif what == "mix":
                            mix_vector(i, s)
                    if stage == "zg" and n == 0:
                        vg_norm(i)
                    if stage == "zg" and n == 1:
                        vg_scale(i)
                    if stage == "brg":
                        dve.wait_ge(mhi_ready, 8 * i + index + 1)
                        dve.tensor_tensor(mlo[:, index, :], gac[:, n, :], mhi[:, index, :], ALU.subtract)\
                           .then_inc(mlo_ready, 1)
                dve.wait_ge(mean_used, 8 * i + 8)
                for k in range(KT):
                    dve.tensor_tensor(h[:, k, META:T], h[:, k, META:T], aux[:, 1, :], ALU.subtract)\
                       .then_inc(xc_ready, 1)
                dve.wait_ge(sq_used, 24 + 8 * i + 8)
                inverse_vector(dve, 3 + i, aux[:, 0, :], rstd[:, 0:SEQ], LN_EPS, SEQ)

                for k in range(KT + 1):
                    if k < KT:
                        dve.tensor_tensor(h[:, k, META:T], h[:, k, META:T], rstd[:, 0:SEQ], ALU.mult)\
                           .then_inc(ln_t, 1)
                    if k:
                        dve.wait_ge(ln_t, 8 * i + k)
                        dve.tensor_scalar(h[:, k - 1, META:T], h[:, k - 1, META:T],
                                          vec2[:, bass.ds(LNG + 8 * i + k - 1, 1)],
                                          vec2[:, bass.ds(LNB + 8 * i + k - 1, 1)], ALU.mult, ALU.add)\
                           .then_inc(xn_ready, 1)


_INS = ["x", "meta_tokens", "norm_w", "pool_w_in", "pool_w_grp", "pool_scale", "pool_w_out", "hgrn_w_in",
        "hgrn_lb_logits", "hgrn_o_norm", "hgrn_w_out", "final_norm_w", "w_in_2", "b_in_2", "attn_sinks_2",
        "gmlp_ln_g_2", "gmlp_ln_b_2", "w_spatial_2", "b_spatial_2", "w_branch_attn_2", "w_branch_gmlp_2",
        "w_out_2", "b_out_2", "ln_g_2", "ln_b_2"]


def shape_constants(np):
    pool = np.zeros((P, NG, 20), np.float32)
    for g, w in enumerate((2, 4, 8, 16)):
        pool[:, g, 0:3] = [w >= 4, w >= 8, w >= 16]
        pool[:, g, 3] = 1.0 / w
        pool[:, g, 4:20] = w / np.minimum(np.arange(16) + 1, w)
    s = np.arange(P)[:, None]
    masks = [s == np.arange(P)[None, :]]
    for level in range(MASKED):
        m = 2 ** level
        t = np.array([t for t in range(P) if t & m])[None, :]
        masks.append((s // (2 * m) == t // (2 * m)) & (s & m == 0))
    dist = np.arange(P)[:, None] + P - np.arange(2 * P)[None, :]
    nd = np.where((dist >= 0) & (dist < P), -dist, -1e30)
    return {"c_ident": np.eye(P, dtype=np.float32), "c_pool": pool,
            "c_masks": np.concatenate(masks, 1).astype(np.int32), "c_nd": nd.astype(np.float32),
            "c_causal": (s <= np.arange(P)[None, :]).astype(np.float32)}


def kernel(**inputs):
    import numpy as np
    import concourse.bacc as bacc
    from concourse import mybir as _mybir
    from concourse.bass_utils import run_bass_kernel_spmd as run

    nc = bacc.Bacc("TRN2", target_bir_lowering=False, num_devices=1)
    arrays, args = {}, {}
    for name, value in [(n, inputs[n]) for n in _INS] + list(shape_constants(np).items()):
        x = np.ascontiguousarray(value)
        arrays[f"in_{name}"] = x
        args[name] = nc.dram_tensor(f"in_{name}", x.shape, _mybir.dt.from_np(x.dtype), kind="ExternalInput").ap()
    out = nc.dram_tensor("out_0", (1, SEQ, D), F32, kind="ExternalOutput").ap()
    program(nc, args, out)
    r = run(nc, [arrays], core_ids=[0])
    return r.results[0]["out_0"]
```
